# Optimizing a Trainium2 kernel written in Bass

```python
import jax, jax.numpy as jnp
from jax import lax
import numpy as np

D_MODEL = 1024
BATCH = 1
SEQ = 256
DEPTH = 2

N_MIXERS = 2
N_A = (DEPTH + 1) // 2
N_B = DEPTH // 2
EPS = 1e-6

A_HEADS = 4
A_DQK = D_MODEL // 8
A_DV = D_MODEL // 4
A_CHUNK = 64
A_TOK = 2 * A_HEADS * A_DQK + 2 * A_HEADS * A_DV + 2 * A_HEADS

B_HEADS = 16
B_KV_HEADS = 2
B_GROUP = B_HEADS // B_KV_HEADS
B_HD = D_MODEL // 16
B_WINDOW = 128
B_BLOCK = 128
B_TOK = (B_HEADS + 2 * B_KV_HEADS) * B_HD
ROT_DIM = B_HD // 4
ROPE_THETA = 500000.0

N_MEM = 256
M_HEADS = 4
M_HD = D_MODEL // 8
M_Q = M_HEADS * M_HD

A_IN = A_TOK + M_Q
B_IN = B_TOK + M_Q
A_OUT = A_HEADS * A_DV + M_Q
B_OUT = B_HEADS * B_HD + M_Q

D_FF = 256 * ((8 * D_MODEL // 3 + 255) // 256)


def rms_norm(x, g):
    xf = x.astype(jnp.float32)
    y = xf * lax.rsqrt(jnp.mean(xf * xf, axis=-1, keepdims=True) + EPS)
    return (y * g.astype(jnp.float32)).astype(x.dtype)

def swiglu(x, w_in, w_out):
    gate, up = jnp.split(x @ w_in, 2, axis=-1)
    return (jax.nn.silu(gate) * up) @ w_out

def rope_tables(positions):
    inv_freq = ROPE_THETA ** (-jnp.arange(0, ROT_DIM, 2, dtype=jnp.float32) / ROT_DIM)
    ang = positions.astype(jnp.float32)[..., None] * inv_freq
    return jnp.cos(ang), jnp.sin(ang)

def apply_partial_rope(x, cos, sin):
    half = ROT_DIM // 2
    x1, x2, rest = x[..., :half], x[..., half:ROT_DIM], x[..., ROT_DIM:]
    c, s = cos[:, :, None, :], sin[:, :, None, :]
    return jnp.concatenate([x1 * c - x2 * s, x2 * c + x1 * s, rest], axis=-1)

def mlstm_chunkwise(q, k, v, i_pre, logf):
    bsz, nh, t, dk = q.shape
    dv = v.shape[-1]
    nc = t // A_CHUNK

    def chunks(a):
        a = a.reshape(a.shape[:2] + (nc, A_CHUNK) + a.shape[3:])
        return jnp.moveaxis(a, 2, 0)

    causal = jnp.tril(jnp.ones((A_CHUNK, A_CHUNK), dtype=bool))

    def step(carry, inp):
        c_st, n_st, m_st = carry
        qc, kc, vc, ic, fc = inp
        b = jnp.cumsum(fc, axis=-1)
        log_d = b[..., :, None] - b[..., None, :] + ic[..., None, :]
        log_d = jnp.where(causal, log_d, -jnp.inf)
        m_inter = b + m_st[..., None]
        m_t = jnp.maximum(m_inter, jnp.max(log_d, axis=-1))
        s = jnp.einsum('bhjd,bhsd->bhjs', qc, kc) * jnp.exp(log_d - m_t[..., None])
        inter = jnp.exp(m_inter - m_t)
        num = (jnp.einsum('bhjs,bhsv->bhjv', s, vc)
               + inter[..., None] * jnp.einsum('bhjd,bhvd->bhjv', qc, c_st))
        den = jnp.sum(s, axis=-1) + inter * jnp.einsum('bhjd,bhd->bhj', qc, n_st)
        h = num / jnp.maximum(jnp.abs(den), jnp.exp(-m_t))[..., None]
        b_last = b[..., -1]
        log_w = b_last[..., None] - b + ic
        m_new = jnp.maximum(b_last + m_st, jnp.max(log_w, axis=-1))
        w = jnp.exp(log_w - m_new[..., None])
        decay = jnp.exp(b_last + m_st - m_new)
        c_new = decay[..., None, None] * c_st + jnp.einsum('bhsv,bhsd->bhvd', w[..., None] * vc, kc)
        n_new = decay[..., None] * n_st + jnp.einsum('bhs,bhsd->bhd', w, kc)
        return (c_new, n_new, m_new), h

    init = (jnp.zeros((bsz, nh, dv, dk), jnp.float32),
            jnp.zeros((bsz, nh, dk), jnp.float32),
            jnp.zeros((bsz, nh), jnp.float32))
    xs = (chunks(q * dk ** -0.5), chunks(k), chunks(v), chunks(i_pre), chunks(logf))
    _, hs = lax.scan(step, init, xs)
    return jnp.moveaxis(hs, 0, 2).reshape(bsz, nh, t, dv)

def mlstm_heads(tok, gate_b, h_norm_g):
    bsz, t, _ = tok.shape
    o1 = A_HEADS * A_DQK
    o2 = 2 * o1
    o3 = o2 + A_HEADS * A_DV
    o4 = o3 + A_HEADS * A_DV
    f32 = jnp.float32
    q = tok[..., :o1].reshape(bsz, t, A_HEADS, A_DQK).transpose(0, 2, 1, 3).astype(f32)
    k = tok[..., o1:o2].reshape(bsz, t, A_HEADS, A_DQK).transpose(0, 2, 1, 3).astype(f32)
    v = tok[..., o2:o3].reshape(bsz, t, A_HEADS, A_DV).transpose(0, 2, 1, 3).astype(f32)
    o_gate = jax.nn.sigmoid(tok[..., o3:o4].astype(f32))
    gates = tok[..., o4:].astype(f32) + gate_b.astype(f32)
    i_pre = gates[..., :A_HEADS].transpose(0, 2, 1)
    logf = jax.nn.log_sigmoid(gates[..., A_HEADS:]).transpose(0, 2, 1)
    h = mlstm_chunkwise(q, k, v, i_pre, logf).transpose(0, 2, 1, 3)
    h = rms_norm(h, h_norm_g.reshape(A_HEADS, A_DV)).reshape(bsz, t, A_HEADS * A_DV)
    return (h * o_gate).astype(tok.dtype)

def swa_heads(tok, cos, sin, q_norm_g, k_norm_g, sinks):
    bsz, t, _ = tok.shape
    f32 = jnp.float32
    nq = B_HEADS * B_HD
    nk = B_KV_HEADS * B_HD
    q = tok[..., :nq].reshape(bsz, t, B_HEADS, B_HD).astype(f32)
    k = tok[..., nq:nq + nk].reshape(bsz, t, B_KV_HEADS, B_HD).astype(f32)
    v = tok[..., nq + nk:].reshape(bsz, t, B_KV_HEADS, B_HD).astype(f32)
    q = apply_partial_rope(rms_norm(q, q_norm_g), cos, sin) * B_HD ** -0.5
    k = apply_partial_rope(rms_norm(k, k_norm_g), cos, sin)
    nb = t // B_BLOCK
    qb = q.reshape(bsz, nb, B_BLOCK, B_KV_HEADS, B_GROUP, B_HD)
    kb = k.reshape(bsz, nb, B_BLOCK, B_KV_HEADS, B_HD)
    vb = v.reshape(bsz, nb, B_BLOCK, B_KV_HEADS, B_HD)

    def band(a):
        prev = jnp.concatenate([jnp.zeros_like(a[:, :1]), a[:, :-1]], axis=1)
        return jnp.moveaxis(jnp.concatenate([prev, a], axis=2), 1, 0)

    qi = jnp.arange(B_BLOCK)[:, None]
    kj = jnp.arange(2 * B_BLOCK)[None, :]
    diff = B_BLOCK + qi - kj
    in_window = (diff >= 0) & (diff < B_WINDOW)
    sink = sinks.astype(f32).reshape(B_KV_HEADS, B_GROUP)[None, :, :, None, None]

    def block(args):
        n, qn, kn, vn = args
        valid = in_window & ((n * B_BLOCK - B_BLOCK + kj) >= 0)
        s = jnp.einsum('bqhgd,bkhd->bhgqk', qn, kn)
        s = jnp.where(valid, s, -jnp.inf)
        m = jnp.maximum(jnp.max(s, axis=-1, keepdims=True), sink)
        p = jnp.exp(s - m)
        denom = jnp.sum(p, axis=-1, keepdims=True) + jnp.exp(sink - m)
        return jnp.einsum('bhgqk,bkhd->bqhgd', p / denom, vn)

    out = lax.map(block, (jnp.arange(nb), jnp.moveaxis(qb, 1, 0), band(kb), band(vb)))
    return jnp.moveaxis(out, 0, 1).reshape(bsz, t, nq).astype(tok.dtype)

def memory_heads(xq, mem_k, mem_v, q_norm_g, k_norm_g):
    bsz, t, _ = xq.shape
    f32 = jnp.float32
    q = rms_norm(xq.reshape(bsz, t, M_HEADS, M_HD).astype(f32), q_norm_g)
    k = rms_norm(mem_k.astype(f32), k_norm_g)
    s = jnp.einsum('bthd,bmhd->bhtm', q, k) * M_HD ** -0.5
    p = jax.nn.softmax(s, axis=-1)
    o = jnp.einsum('bhtm,bmhd->bthd', p, mem_v.astype(f32))
    return o.reshape(bsz, t, M_Q).astype(xq.dtype)

def first_inputs(seed: int = 0) -> dict:
    key = jax.random.key(seed)
    ks = jax.random.split(key, 32)
    f32 = jnp.float32

    def normal(k, shape, scale):
        return jax.random.normal(k, shape, f32) * scale

    def gain(k, shape):
        return 1.0 + 0.05 * jax.random.normal(k, shape, f32)

    x = normal(ks[0], (BATCH, SEQ, D_MODEL), 1.0)
    mem = normal(ks[1], (BATCH, N_MEM, D_MODEL), 1.0)
    start = jax.random.randint(ks[2], (BATCH, 1), 0, 4096, dtype=jnp.int32)
    positions = start + jnp.arange(SEQ, dtype=jnp.int32)[None, :]
    i_bias = normal(ks[3], (N_A, A_HEADS), 0.1)
    f_bias = jnp.linspace(3.0, 6.0, A_HEADS, dtype=f32)[None, :] + normal(ks[4], (N_A, A_HEADS), 0.1)
    return {
        'x': x,
        'mem': mem,
        'positions': positions,
        'mem_norm_g': gain(ks[5], (D_MODEL,)),
        'mem_w_kv': normal(ks[6], (D_MODEL, 2 * M_Q), D_MODEL ** -0.5),
        'ffn1_norm_g': gain(ks[7], (DEPTH, D_MODEL)),
        'ffn1_w_in': normal(ks[8], (DEPTH, D_MODEL, 2 * D_FF), D_MODEL ** -0.5),
        'ffn1_w_out': normal(ks[9], (DEPTH, D_FF, D_MODEL), 0.5 * D_FF ** -0.5),
        'mix_norm_g': gain(ks[10], (DEPTH, D_MODEL)),
        'ffn2_norm_g': gain(ks[11], (DEPTH, D_MODEL)),
        'ffn2_w_in': normal(ks[12], (DEPTH, D_MODEL, 2 * D_FF), D_MODEL ** -0.5),
        'ffn2_w_out': normal(ks[13], (DEPTH, D_FF, D_MODEL), 0.5 * D_FF ** -0.5),
        'xa_q_norm_g': gain(ks[14], (DEPTH, M_HD)),
        'xa_k_norm_g': gain(ks[15], (DEPTH, M_HD)),
        'a_w_in': normal(ks[16], (N_A, D_MODEL, A_IN), D_MODEL ** -0.5),
        'a_gate_b': jnp.concatenate([i_bias, f_bias], axis=-1),
        'a_h_norm_g': gain(ks[17], (N_A, A_HEADS * A_DV)),
        'a_w_out': normal(ks[18], (N_A, A_OUT, D_MODEL), 0.5 * A_OUT ** -0.5),
        'b_w_in': normal(ks[19], (N_B, D_MODEL, B_IN), D_MODEL ** -0.5),
        'b_q_norm_g': gain(ks[20], (N_B, B_HD)),
        'b_k_norm_g': gain(ks[21], (N_B, B_HD)),
        'b_sinks': normal(ks[22], (N_B, B_HEADS), 0.5),
        'b_w_out': normal(ks[23], (N_B, B_OUT, D_MODEL), 0.5 * B_OUT ** -0.5),
    }

def first_block(x, mem, positions, mem_norm_g, mem_w_kv, ffn1_norm_g, ffn1_w_in, ffn1_w_out,
              mix_norm_g, ffn2_norm_g, ffn2_w_in, ffn2_w_out, xa_q_norm_g, xa_k_norm_g,
              a_w_in, a_gate_b, a_h_norm_g, a_w_out,
              b_w_in, b_q_norm_g, b_k_norm_g, b_sinks, b_w_out):
    bsz, n_mem, _ = mem.shape
    mem_kv = rms_norm(mem, mem_norm_g) @ mem_w_kv
    mem_k = mem_kv[..., :M_Q].reshape(bsz, n_mem, M_HEADS, M_HD)
    mem_v = mem_kv[..., M_Q:].reshape(bsz, n_mem, M_HEADS, M_HD)
    cos, sin = rope_tables(positions)
    for i in range(DEPTH):
        j = i // N_MIXERS
        x = x + 0.5 * swiglu(rms_norm(x, ffn1_norm_g[i]), ffn1_w_in[i], ffn1_w_out[i])
        hn = rms_norm(x, mix_norm_g[i])
        if i % N_MIXERS == 0:
            proj = hn @ a_w_in[j]
            y_tok = mlstm_heads(proj[..., :A_TOK], a_gate_b[j], a_h_norm_g[j])
            xq = proj[..., A_TOK:]
            w_out = a_w_out[j]
        else:
            proj = hn @ b_w_in[j]
            y_tok = swa_heads(proj[..., :B_TOK], cos, sin, b_q_norm_g[j], b_k_norm_g[j], b_sinks[j])
            xq = proj[..., B_TOK:]
            w_out = b_w_out[j]
        y_mem = memory_heads(xq, mem_k, mem_v, xa_q_norm_g[i], xa_k_norm_g[i])
        x = x + jnp.concatenate([y_tok, y_mem], axis=-1) @ w_out
        x = x + 0.5 * swiglu(rms_norm(x, ffn2_norm_g[i]), ffn2_w_in[i], ffn2_w_out[i])
    return x


DEPTH_2 = 1

CHUNK = 64
SSD_EXPAND = 2
SSD_INNER = SSD_EXPAND * D_MODEL
SSD_HEAD_DIM = 64
SSD_HEADS = SSD_INNER // SSD_HEAD_DIM
SSD_GROUPS = 4
SSD_HPG = SSD_HEADS // SSD_GROUPS
SSD_STATE = 128
SSD_CONV = 4
SSD_XBC = SSD_INNER + 2 * SSD_GROUPS * SSD_STATE
SCONV_DIM = D_MODEL
SCONV_K = 3
FFN_HIDDEN = ((8 * D_MODEL + 767) // 768) * 256
IN_SIZES = (SSD_INNER, SSD_XBC, SSD_HEADS, SCONV_DIM, SCONV_DIM, SCONV_DIM, D_MODEL, D_MODEL)
IN_DIM = sum(IN_SIZES)
IN_SPLITS = tuple(int(v) for v in np.cumsum(IN_SIZES)[:-1])


def rmsnorm(x, w):
    x32 = x.astype(jnp.float32)
    y = x32 * lax.rsqrt(jnp.mean(x32 * x32, axis=-1, keepdims=True) + EPS)
    return (y * w.astype(jnp.float32)).astype(x.dtype)

def causal_depthwise_conv(x, w):
    k = w.shape[0]
    return lax.conv_general_dilated(
        x, w[:, None, :].astype(x.dtype), window_strides=(1,), padding=[(k - 1, 0)],
        dimension_numbers=('NWC', 'WIO', 'NWC'), feature_group_count=x.shape[-1])

def ssd_chunked_scan(x, dt, a, bm, cm):
    bsz, seqlen = x.shape[0], x.shape[1]
    nc = seqlen // CHUNK

    def to_chunks(t):
        return jnp.moveaxis(t.reshape((bsz, nc, CHUNK) + t.shape[2:]), 1, 0)

    causal = jnp.tril(jnp.ones((CHUNK, CHUNK), dtype=bool))[None, :, :, None, None]

    def step(state, inp):
        xc, dtc, bc, cc = inp
        acum = jnp.cumsum(dtc * a, axis=1)
        seg = acum[:, :, None] - acum[:, None, :]
        decay = jnp.exp(jnp.where(causal, seg, -jnp.inf))
        cb = jnp.einsum('blgn,bsgn->blsg', cc, bc)
        xdt = xc * dtc[..., None]
        scores = cb[..., None] * decay
        y_diag = jnp.einsum('blsgr,bsgrp->blgrp', scores, xdt)
        y_off = jnp.einsum('blgn,bgrpn->blgrp', cc, state) * jnp.exp(acum)[..., None]
        to_end = jnp.exp(acum[:, -1:] - acum)
        new_state = (state * jnp.exp(acum[:, -1])[..., None, None]
                     + jnp.einsum('bsgn,bsgr,bsgrp->bgrpn', bc, to_end, xdt))
        return new_state, y_diag + y_off

    state0 = jnp.zeros((bsz, SSD_GROUPS, SSD_HPG, SSD_HEAD_DIM, SSD_STATE), jnp.float32)
    _, ys = lax.scan(step, state0, (to_chunks(x), to_chunks(dt), to_chunks(bm), to_chunks(cm)))
    return jnp.moveaxis(ys, 0, 1).reshape(x.shape)

def hybrid_mixer(h, w_in, ssd_conv_w, ssd_conv_b, dt_bias, a_log, d_skip, ssd_norm_w,
                 w_ssd_proj, sconv_w, w_sconv_proj, w_o):
    bsz, seqlen, _ = h.shape
    u = h @ w_in
    z, xbc, dt_raw, s_b, s_c, s_x, g_a, g_b = jnp.split(u, IN_SPLITS, axis=-1)

    xbc = jax.nn.silu(causal_depthwise_conv(xbc, ssd_conv_w) + ssd_conv_b)
    xs, bm, cm = jnp.split(xbc, (SSD_INNER, SSD_INNER + SSD_GROUPS * SSD_STATE), axis=-1)
    xs32 = xs.astype(jnp.float32).reshape(bsz, seqlen, SSD_GROUPS, SSD_HPG, SSD_HEAD_DIM)
    dt = jax.nn.softplus(dt_raw.astype(jnp.float32) + dt_bias.astype(jnp.float32))
    dt = dt.reshape(bsz, seqlen, SSD_GROUPS, SSD_HPG)
    a = -jnp.exp(a_log.astype(jnp.float32)).reshape(SSD_GROUPS, SSD_HPG)
    bm32 = bm.astype(jnp.float32).reshape(bsz, seqlen, SSD_GROUPS, SSD_STATE)
    cm32 = cm.astype(jnp.float32).reshape(bsz, seqlen, SSD_GROUPS, SSD_STATE)
    y = ssd_chunked_scan(xs32, dt, a, bm32, cm32)
    y = y + d_skip.astype(jnp.float32).reshape(SSD_GROUPS, SSD_HPG)[..., None] * xs32
    y = y.reshape(bsz, seqlen, SSD_INNER) * jax.nn.silu(z.astype(jnp.float32))
    yg = y.reshape(bsz, seqlen, SSD_GROUPS, SSD_INNER // SSD_GROUPS)
    yg = yg * lax.rsqrt(jnp.mean(yg * yg, axis=-1, keepdims=True) + EPS)
    y = (yg.reshape(bsz, seqlen, SSD_INNER) * ssd_norm_w.astype(jnp.float32)).astype(h.dtype)
    branch_a = y @ w_ssd_proj

    v = causal_depthwise_conv(s_c * s_x, sconv_w)
    branch_b = (s_b * v) @ w_sconv_proj

    merged = jax.nn.sigmoid(g_a) * branch_a + jax.nn.sigmoid(g_b) * branch_b
    return merged @ w_o

def swiglu_2(h, w_gate, w_up, w_down):
    return (jax.nn.silu(h @ w_gate) * (h @ w_up)) @ w_down

def second_inputs(seed: int = 0) -> dict:
    key = jax.random.key(seed)
    ks = jax.random.split(key, 20)
    f32 = jnp.float32

    def nrm(k, shape, scale):
        return jax.random.normal(k, shape, f32) * scale

    x = jax.random.normal(ks[0], (BATCH, SEQ, D_MODEL), f32)
    dt_init = jnp.exp(jax.random.uniform(ks[5], (DEPTH_2, SSD_HEADS), f32, np.log(1e-3), np.log(1e-1)))
    dt_bias = dt_init + jnp.log(-jnp.expm1(-dt_init))
    return {
        'x': x,
        'norm_mix_w': 1.0 + nrm(ks[1], (DEPTH_2, D_MODEL), 0.05),
        'w_in': nrm(ks[2], (DEPTH_2, D_MODEL, IN_DIM), D_MODEL ** -0.5),
        'ssd_conv_w': nrm(ks[3], (DEPTH_2, SSD_CONV, SSD_XBC), SSD_CONV ** -0.5),
        'ssd_conv_b': nrm(ks[4], (DEPTH_2, SSD_XBC), 0.01),
        'dt_bias': dt_bias,
        'a_log': jnp.log(jax.random.uniform(ks[6], (DEPTH_2, SSD_HEADS), f32, 1.0, 16.0)),
        'd_skip': 1.0 + nrm(ks[7], (DEPTH_2, SSD_HEADS), 0.1),
        'ssd_norm_w': 1.0 + nrm(ks[8], (DEPTH_2, SSD_INNER), 0.05),
        'w_ssd_proj': nrm(ks[9], (DEPTH_2, SSD_INNER, D_MODEL), SSD_INNER ** -0.5),
        'sconv_w': nrm(ks[10], (DEPTH_2, SCONV_K, SCONV_DIM), SCONV_K ** -0.5),
        'w_sconv_proj': nrm(ks[11], (DEPTH_2, SCONV_DIM, D_MODEL), SCONV_DIM ** -0.5),
        'w_o': nrm(ks[12], (DEPTH_2, D_MODEL, D_MODEL), D_MODEL ** -0.5),
        'norm_ffn_w': 1.0 + nrm(ks[13], (DEPTH_2, D_MODEL), 0.05),
        'w_gate': nrm(ks[14], (DEPTH_2, D_MODEL, FFN_HIDDEN), D_MODEL ** -0.5),
        'w_up': nrm(ks[15], (DEPTH_2, D_MODEL, FFN_HIDDEN), D_MODEL ** -0.5),
        'w_down': nrm(ks[16], (DEPTH_2, FFN_HIDDEN, D_MODEL), FFN_HIDDEN ** -0.5),
        'final_norm_w': 1.0 + nrm(ks[17], (D_MODEL,), 0.05),
    }

def second_block(x, norm_mix_w, w_in, ssd_conv_w, ssd_conv_b, dt_bias, a_log, d_skip, ssd_norm_w,
              w_ssd_proj, sconv_w, w_sconv_proj, w_o, norm_ffn_w, w_gate, w_up, w_down,
              final_norm_w):
    h = x
    for i in range(DEPTH_2):
        h = h + hybrid_mixer(rmsnorm(h, norm_mix_w[i]), w_in[i], ssd_conv_w[i], ssd_conv_b[i],
                             dt_bias[i], a_log[i], d_skip[i], ssd_norm_w[i], w_ssd_proj[i],
                             sconv_w[i], w_sconv_proj[i], w_o[i])
        h = h + swiglu_2(rmsnorm(h, norm_ffn_w[i]), w_gate[i], w_up[i], w_down[i])
    return rmsnorm(h, final_norm_w)


def setup_inputs(seed=0):
    out = dict(first_inputs(seed))
    for name, value in second_inputs(seed + 1).items():
        if name != "x":
            out[name + "_2"] = value
    return out


def reference(
    x, mem, positions, mem_norm_g, mem_w_kv, ffn1_norm_g, ffn1_w_in, ffn1_w_out, mix_norm_g,
    ffn2_norm_g, ffn2_w_in, ffn2_w_out, xa_q_norm_g, xa_k_norm_g, a_w_in, a_gate_b, a_h_norm_g,
    a_w_out, b_w_in, b_q_norm_g, b_k_norm_g, b_sinks, b_w_out, norm_mix_w_2, w_in_2,
    ssd_conv_w_2, ssd_conv_b_2, dt_bias_2, a_log_2, d_skip_2, ssd_norm_w_2, w_ssd_proj_2,
    sconv_w_2, w_sconv_proj_2, w_o_2, norm_ffn_w_2, w_gate_2, w_up_2, w_down_2, final_norm_w_2,
):
    x = first_block(
        x, mem, positions, mem_norm_g, mem_w_kv, ffn1_norm_g, ffn1_w_in, ffn1_w_out, mix_norm_g,
        ffn2_norm_g, ffn2_w_in, ffn2_w_out, xa_q_norm_g, xa_k_norm_g, a_w_in, a_gate_b,
        a_h_norm_g, a_w_out, b_w_in, b_q_norm_g, b_k_norm_g, b_sinks, b_w_out,
    )
    return second_block(
        x, norm_mix_w_2, w_in_2, ssd_conv_w_2, ssd_conv_b_2, dt_bias_2, a_log_2, d_skip_2,
        ssd_norm_w_2, w_ssd_proj_2, sconv_w_2, w_sconv_proj_2, w_o_2, norm_ffn_w_2, w_gate_2,
        w_up_2, w_down_2, final_norm_w_2,
    )


_drawn_inputs = setup_inputs


def setup_inputs(seed=0):
    import zlib

    import numpy as np

    out = dict(_drawn_inputs(seed))
    spreads = {}
    factors = {'mem_norm_g': 8.0,
     'ffn2_norm_g': 2.892,
     'xa_q_norm_g': 8.0,
     'xa_k_norm_g': 8.0,
     'a_h_norm_g': 3.782,
     'b_q_norm_g': 8.0,
     'b_k_norm_g': 8.0,
     'b_sinks': 200.0,
     'ssd_conv_b_2': 30.692,
     'norm_mix_w_2': 3.495,
     'd_skip_2': 57.0,
     'ssd_norm_w_2': 41.845,
     'norm_ffn_w_2': 5.353}
    for name, (base, spread) in spreads.items():
        noise = np.random.default_rng([zlib.crc32(name.encode()), seed]).standard_normal(out[name].shape)
        drawn = base * np.exp(spread * noise) if base else spread * noise
        out[name] = __import__('jax').numpy.asarray(drawn.astype(out[name].dtype))
    for name, factor in factors.items():
        out[name] = (out[name] * factor).astype(out[name].dtype)
    return out
```

```python
from contextlib import ExitStack

import concourse.bass as bass
import numpy as np
from concourse import mybir

F32 = mybir.dt.float32
F32R = mybir.dt.float32r
I32 = mybir.dt.int32
ALU = mybir.AluOpType
ACT = mybir.ActivationFunctionType
AXX = mybir.AxisListType.X

P = 128
T = 256
D = 1024
DT = D // P
FF = 2816
NI = FF // 256
RING = 3
UNIT = 2048
EPS = 1e-6
NEG = -1e30
A_HD, M_HD, B_HD = 128, 128, 64
A_TOK, A_GATES = 3080, 3072
B_TOK = 1280
A_OUT = 1536
SSD_XBC, SSD_DT, SSD_SB, SSD_SC, SSD_SX, SSD_GA, SSD_GB = 2048, 5120, 5152, 6176, 7200, 8224, 9248
SETS = {"lnexp": "natural_log_exp_and_others", "silu": "silu_and_others", "exp": "exp_and_others"}


class Count:

    def __init__(self, known):
        self.n, self.known, self.found = 0, known, {}

    def __call__(self, step):
        self.n += 1
        assert step not in self.found, step
        self.found[step] = self.n
        return 1

    def at(self, step):
        return self.known[step] if self.known else 1


def plan_units():
    first, opens = {}, []

    def add(name, pattern):
        first[name] = len(opens)
        opens.extend(c == "g" for c in pattern)

    ffn = "gg" + "ggd" * (NI - 1) + "d"
    add("mem", "gggg")
    add("ffn0", ffn)
    add("mixa", "g" * 15)
    add("mixa_out", "d" * (A_OUT // 256))
    add("ffn1", ffn)
    add("ffn2", ffn)
    add("mixb", "g" * 7)
    add("mixb_out", "d" * (A_OUT // 256))
    add("ffn3", ffn)
    add("dt", "g")
    add("bc", "gggg")
    add("xs", "g" * 8)
    add("z", "g" * 8)
    add("ga", "gggg")
    add("gb", "gggg")
    add("aproj", "gd" * 4)
    add("sconv", "ggg" * 4)
    add("sproj", "gggg")
    add("w_o", "dddd")
    add("ffn4", ffn)
    return first, opens


def build(nc, a, out, known=None):
    U, OPENS = plan_units()
    NU = len(OPENS)
    fills = [sum(OPENS[v] for v in range(u + 1) if v % RING == u % RING) for u in range(NU)]
    counts = {e: Count((known or {}).get(e)) for e in ("vec", "act", "pe", "pool", "root")}
    vec, act_, pe_, pool_, root_ = (counts[e] for e in ("vec", "act", "pe", "pool", "root"))

    with ExitStack() as ctx:
        def sb(name, shape, dt=F32):
            return ctx.enter_context(nc.sbuf_tensor(name, shape, dt))

        def sem(name):
            return ctx.enter_context(nc.semaphore(name))

        w_raw = sb("w_raw", [P, RING, UNIT])
        w_hi = sb("w_hi", [P, RING, UNIT], F32R)
        w_lo = sb("w_lo", [P, RING, UNIT], F32R)
        x = sb("x", [P, DT, T])
        xg_hi = sb("xg_hi", [P, DT, T], F32R)
        xg_lo = sb("xg_lo", [P, DT, T], F32R)
        y_hi = sb("y_hi", [P, 16, T], F32R)
        y_lo = sb("y_lo", [P, 16, T], F32R)
        rstd = sb("rstd", [P, T])
        rs_v = sb("rs_v", [P, T])
        rs_y = sb("rs_y", [P, T])
        rs_t = sb("rs_t", [P, T])
        ident = sb("ident", [P, P])
        ones = sb("ones", [P, P])
        cols = sb("cols", [P, 3, P])
        mask = sb("mask", [P, 384])
        window = sb("window", [P, 384])
        block_ones = sb("block_ones", [P, P])
        rotate = sb("rotate", [P, P])
        swap = sb("swap", [P, P])
        pair_rows = sb("pair_rows", [P, 32])
        head_rows = sb("head_rows", [P, 4, 4])
        gate_bias = sb("gate_bias", [4, 2])
        sinks = sb("sinks", [P, 16])
        inv_freq = sb("inv_freq", [P, 1])
        gain_qk = sb("gain_qk", [P, 2])
        gain_b = sb("gain_b", [P, 2])
        rope = sb("rope", [P, 2, T])
        small = sb("small", [P, 64])
        mem_k = sb("mem_k", [P, 4, T])
        mem_v = sb("mem_v", [P, 2, 512])
        scr = sb("scr", [P, 14336])
        ps = ctx.enter_context(nc.psum_tensor("ps", [P, 8, 512], F32))
        STAT = 7

        def KB(at, size):
            return scr[:, int(at * 256):int((at + size) * 256)]

        def tiles(ap, n=T):
            return ap.rearrange("p (k t) -> p k t", t=n)

        rows = tiles(KB(44, 1.5), P)
        pos = KB(39, 1).bitcast(I32)
        sq = tiles(KB(0, 8), 512)
        gate_s, up_s = KB(8, 2), KB(10, 2)
        xin = tiles(KB(16, 8), D)
        memin = tiles(KB(24, 8), D)
        x_gain = tiles(KB(8, 8))
        fin_r, fin_v, fin_t = small[:, 0:2], small[:, 2:4], small[:, 4:6]
        mem_t = tiles(KB(8, 8))
        yout = tiles(KB(16, 8), D)

        w_landed = [sem(f"w_landed{s}") for s in range(RING)]
        w_rounded = sem("w_rounded")
        w_split = sem("w_split")
        w_used = sem("w_used")
        drained = [sem(f"drained{b}") for b in range(RING)]
        loaded = sem("loaded")
        gain_loaded = sem("gain_loaded")
        x_loaded, mem_loaded = sem("x_loaded"), sem("mem_loaded")
        stored = sem("stored")
        acc_ready = sem("acc_ready")
        turned = sem("turned")
        x_new = sem("x_new")
        xh_ready, xl_ready = sem("xh_ready"), sem("xl_ready")
        squared, sq_summed, stat_done = sem("squared"), sem("sq_summed"), sem("stat_done")
        rs_vec, rs_act = sem("rs_vec"), sem("rs_act")
        ffn_silu, ffn_h, ffn_hh, ffn_hl = (sem(n) for n in ("ffn_silu", "ffn_h", "ffn_hh", "ffn_hl"))
        vec_done, act_done, pe_done, pool_done = (sem(n) for n in ("vec_done", "act_done", "pe_done", "pool_done"))

        def g_src(w, c):
            return w.rearrange("(k p) c -> p k c", p=P)[:, :, bass.ds(c, 256)]

        def d_src(w, r):
            return w[bass.ds(r, 256), :].rearrange("(k p) c -> p k c", p=P)

        FFNS = [(a["ffn1_w_in"][0], a["ffn1_w_out"][0]), (a["ffn2_w_in"][0], a["ffn2_w_out"][0]),
                (a["ffn1_w_in"][1], a["ffn1_w_out"][1]), (a["ffn2_w_in"][1], a["ffn2_w_out"][1]), None]

        def ffn_src(f, kind, i):
            if f == 4:
                w = {"g": a["w_gate_2"][0], "u": a["w_up_2"][0], "d": a["w_down_2"][0]}[kind]
                return d_src(w, i * 256) if kind == "d" else g_src(w, i * 256)
            w_in, w_out = FFNS[f]
            if kind == "d":
                return d_src(w_out, i * 256)
            return g_src(w_in, i * 256 + (FF if kind == "u" else 0))

        GAIN = {}
        vec_rows = []

        def vector(name, ap, n, tile=0):
            at = sum(v[2] for v in vec_rows if v[3] == tile)
            vec_rows.append((at, ap, n, tile))
            for k, part in enumerate(name if isinstance(name, tuple) else (name,)):
                GAIN[part] = (tile, at + k * n // (len(name) if isinstance(name, tuple) else 1))

        def r128(ap):
            return ap.rearrange("(k p) -> k p", p=P)

        def m128(ap):
            return ap.rearrange("l (k p) -> (l k) p", p=P)

        vector("mem", r128(a["mem_norm_g"]), 8)
        vector(("ffn0", "ffn2"), m128(a["ffn1_norm_g"]), 16)
        vector(("ffn1", "ffn3"), m128(a["ffn2_norm_g"]), 16)
        vector(("mix0", "mix1"), m128(a["mix_norm_g"]), 16)
        vector("ssd", r128(a["norm_mix_w_2"][0]), 8)
        vector("ffn4", r128(a["norm_ffn_w_2"][0]), 8)
        vector("final", r128(a["final_norm_w_2"]), 8)
        vector("h_norm", r128(a["a_h_norm_g"][0]), 8)
        vector(("xa_q0", "xa_q1"), a["xa_q_norm_g"], 2)
        vector(("xa_k0", "xa_k1"), a["xa_k_norm_g"], 2)
        vector("b_q", a["b_q_norm_g"], 1)
        vector("b_k", a["b_k_norm_g"], 1)

        vector(tuple(f"sconv_w{k}" for k in range(3)), m128(a["sconv_w_2"][0]), 24)
        vector(tuple(f"conv_w{k}" for k in range(4)), m128(a["ssd_conv_w_2"][0]), 96, 1)
        vector("conv_b", r128(a["ssd_conv_b_2"][0]), 24, 1)
        vector("ssd_norm", r128(a["ssd_norm_w_2"][0]), 16, 2)

        N_SMALL = sum(P // v[1].shape[1] for v in vec_rows[1:]) + 8

        def col(name, k=0):
            tile, at = GAIN[name]
            return cols[:, tile, at + k:at + k + 1]

        PHASES = [("mem", "mem", None), ("ffn0", "ffn0", None), ("mixa", "mix0", 0.5), ("ffn1", "ffn1", 1.0),
                  ("ffn2", "ffn2", 0.5), ("mixb", "mix1", 0.5), ("ffn3", "ffn3", 1.0), ("ssd", "ssd", 0.5),
                  ("ffn4", "ffn4", 0.5),
                  ("final", "final", 1.0)]
        LAST = ([p[0] for p in PHASES if p[0].startswith("ffn")] or [""])[-1]
        norm_of = {p[0]: (n, p[1], p[2]) for n, p in enumerate(PHASES)}

        nth = {int(p[0][3:]): k for k, p in enumerate(q for q in PHASES if q[0].startswith("ffn"))}

        a_q, a_k = tiles(KB(0, 4)), tiles(KB(4, 4))
        a_vt, a_v = tiles(KB(8, 8)), tiles(KB(16, 8), D)
        a_e, a_s = tiles(KB(24, 6), 384), tiles(KB(30, 6), 384)
        a_o = tiles(KB(36, 8))
        a_rows = tiles(KB(48, 8))
        GI, GF, GL, LOGF, CUM, GU, GM, GE = range(8)
        a_rden = tiles(KB(0, 4))
        a_h = tiles(KB(8, 8))
        a_hsq = tiles(KB(16, 8))
        u_col = small[:, 0:8]
        xq_a, xsq_a, p_a, pt_a = tiles(KB(44, 4)), tiles(KB(4, 4)), tiles(KB(16, 8)), tiles(KB(0, 8))
        m_stat, m_sum, m_inv, m_r, m_v, m_t = (small[:, 8 * k:8 * k + 8] for k in range(1, 7))
        b_x = tiles(KB(0, 10))
        b_kx = KB(10, 1)
        b_v = tiles(KB(11, 1), P)
        b_sqk, b_rv, b_ry, b_rt = (KB(at, 1) for at in (12, 13, 14, 15))
        b_sq = tiles(KB(36, 8), 512)
        b_sq_tiles = tiles(KB(36, 8))
        b_rows = KB(20, 1)[0:16]
        b_rot = tiles(KB(16, 4), 512)
        b_s = tiles(KB(24, 12), 384)
        b_pt = tiles(KB(36, 6), 384)
        B_STEPS = [(8, 1)] + [(2 * j, 2) for j in range(4)]
        xq_b, xsq_b, p_b, pt_b = tiles(KB(24, 4)), tiles(KB(28, 4)), tiles(KB(44, 8)), tiles(KB(28, 8))
        b_stat = sb("b_stat", [P, 5, 16, 2])
        b_r = sb("b_r", [P, 2, 16])
        b_rvt = small[:, 0:64]
        BLOCKS = ((0, P), (P, 384))

        sc_c, sc_prod, sc_v, sc_b = (tiles(KB(at, 4), 512) for at in (8, 12, 16, 20))
        s_x = tiles(KB(0, 24))
        s_xdt = tiles(KB(24, 16), 2048)
        s_cb = tiles(KB(40, 6), 384)
        s_A = KB(46, 1)[0:32]
        A_hi, A_lo = y_hi[0:32, 0], y_lo[0:32, 0]
        select = sb("select", [32, 32], F32R)
        s_e = tiles(KB(47, 9), 384)
        s_in, s_cv = mem_k, tiles(mem_v[:, :, :].rearrange("p a b -> p (a b)"))
        s_nA, s_dtx, s_dtl, s_dt, s_dA, s_cross, s_dth = (KB(24 + k, 1)[0:32] for k in range(7))
        s_z, s_zth = s_in, s_cv
        s_zsq = tiles(KB(40, 2))
        g_v, g_y, g_t = KB(48, 2), KB(50, 2), KB(52, 2)
        s_gate = tiles(KB(24, 8), 512)
        s_gate_b = [s_in[:, 0:2], s_in[:, 2:4], s_cv[:, 0:2], s_cv[:, 2:4]]
        s_br = tiles(KB(32, 4), 512)
        s_merged = tiles(KB(36, 8))
        ssd_small = sb("ssd_small", [P, 210])
        dt_bias, a_log = ssd_small[0:32, 0:1], ssd_small[0:32, 1:2]
        d_half, d_all = ssd_small[:, 2:18], ssd_small[:, 18:50]
        dt_col = ssd_small[:, 50:114]
        bias_col = ssd_small[:, 114:210]

        uses = [(kind, 4 * b + h) for kind, b in (("S", 0), ("S", 1), ("T", 0), ("T", 1), ("S", 2), ("S", 3), ("T", 2), ("T", 3))
                for h in range(4)]
        BANK = {use: 4 + (U["mixb"] + 4 + k) % RING for k, use in enumerate(uses)}
        BEFORE = {use: uses[k - 3] for k, use in enumerate(uses) if k > 2}

        def rot_bank(j):
            return ps[:, 2 + j % 2, :] if j else ps[:, STAT, :]

        def half(b, h):
            return ps[:, b, (h % 2) * T:(h % 2) * T + T]

        def blocks02(h):
            return s_e[:, h % 6].rearrange("p (b t) -> p b t", b=3)[:, 0::2]

        def conv_tile(c):
            return 16 + 2 * c if c < 4 else 2 * (c - 4)

        def bank(u):
            return 4 + u % RING

        def wide(ap, n=2):
            return ap.unsqueeze(1).broadcast_to([ap.shape[0], n, ap.shape[1]])

        block = ctx.enter_context(nc.Block())

        @block.sync
        def _(sp):
            sp.dma_start(memin, a["mem"][0].rearrange("(k p) d -> p k d", p=P)).then_inc(mem_loaded, 16)
            sp.wait_ge(pool_done, pool_.at("rows 0"))
            sp.dma_start(rows[0:8, 0, :], vec_rows[0][1]).then_inc(gain_loaded, 16)

            def load(u, src, i=0):
                if isinstance(i, int) and u + 6 * i >= NU:
                    return
                if u >= RING:
                    sp.wait_ge(w_split, u - RING + 1 + 6 * i)
                sp.dma_start(w_raw[:, u % RING, :].rearrange("p (k c) -> p k c", k=src.shape[1]),
                             src).then_inc(w_landed[u % RING], 16)

            def ffn(f):
                u = U[f"ffn{f}"]
                load(u, ffn_src(f, "g", 0))
                load(u + 1, ffn_src(f, "u", 0))
                for i in (1, 2):
                    load(u + 3 * i - 1, ffn_src(f, "g", i))
                    load(u + 3 * i, ffn_src(f, "u", i))
                    load(u + 3 * i + 1, ffn_src(f, "d", i - 1))
                with sp.Fori(0, (NI - 3) // 2) as n:
                    for j in range(2):
                        i, v = 3 + j, u + 8 + 3 * j
                        load(v, ffn_src(f, "g", 2 * n + i), n)
                        load(v + 1, ffn_src(f, "u", 2 * n + i), n)
                        load(v + 2, ffn_src(f, "d", 2 * n + i - 1), n)
                load(u + 3 * NI - 1, ffn_src(f, "d", NI - 1))

            def small_inputs():
                for at, ap, n, tile in vec_rows[1:]:
                    w = ap.shape[1]
                    for c in range(0, P, w):
                        sp.dma_start(rows[at:at + n, tile, c:c + w], ap).then_inc(loaded, 16)
                for j in range(2):
                    sp.dma_start(gate_bias[:, j:j + 1], a["a_gate_b"][0][4 * j:4 * j + 4].unsqueeze(1)).then_inc(loaded, 16)
                for dst, src in ((dt_bias, a["dt_bias_2"]), (a_log, a["a_log_2"])):
                    sp.dma_start(dst, src[0].unsqueeze(1)).then_inc(loaded, 16)
                for dst, src in ((sinks[:, :], a["b_sinks"]), (d_all, a["d_skip_2"]), (pos, a["positions"])):
                    sp.dma_start(dst, src[0].partition_broadcast(P)).then_inc(loaded, 16)
                sp.dma_start(inv_freq[:, :], a["inv_freq"]).then_inc(loaded, 16)

            def mem():
                for j in range(3):
                    load(U["mem"] + j, g_src(a["mem_w_kv"], 256 * j))
                sp.dma_start(xin, a["x"][0].rearrange("(k p) d -> p k d", p=P)).then_inc(x_loaded, 16)
                small_inputs()
                load(U["mem"] + 3, g_src(a["mem_w_kv"], 768))

            def mixa():
                for j, c in enumerate([A_GATES] + [256 * k for k in range(12)][:4] + [D + 256 * k for k in range(4)]
                                      + [A_TOK, A_TOK + 256] + [2 * D + 256 * k for k in range(4)]):
                    load(U["mixa"] + j, g_src(a["a_w_in"][0], c))
                for j in range(6):
                    load(U["mixa_out"] + j, d_src(a["a_w_out"][0], 256 * j))

            def mixb():
                for j, c in enumerate([B_TOK, B_TOK + 256, D] + [256 * k for k in range(4)]):
                    load(U["mixb"] + j, g_src(a["b_w_in"][0], c))
                for j, k in enumerate((4, 5, 0, 1, 2, 3)):
                    load(U["mixb_out"] + j, d_src(a["b_w_out"][0], 256 * k))

            def ssd():
                w = a["w_in_2"][0]
                load(U["dt"], g_src(w, SSD_DT))
                for j in range(4):
                    load(U["bc"] + j, g_src(w, SSD_XBC + 2048 + 256 * j))
                for j in range(8):
                    load(U["xs"] + j, g_src(w, SSD_XBC + 256 * j))
                for j in range(8):
                    load(U["z"] + j, g_src(w, 256 * j))
                for j in range(4):
                    load(U["ga"] + j, g_src(w, SSD_GA + 256 * j))
                for j in range(4):
                    load(U["gb"] + j, g_src(w, SSD_GB + 256 * j))
                for j in range(4):
                    for k in range(2):
                        load(U["aproj"] + 2 * j + k, g_src(a["w_ssd_proj_2"][0][D * k:D * k + D], 256 * j))
                for j in range(4):
                    for k, c in enumerate((SSD_SC, SSD_SX, SSD_SB)):
                        load(U["sconv"] + 3 * j + k, g_src(w, c + 256 * j))
                for j in range(4):
                    load(U["sproj"] + j, g_src(a["w_sconv_proj_2"][0], 256 * j))
                for j in range(4):
                    load(U["w_o"] + j, d_src(a["w_o_2"][0], 256 * j))

            for name, _, _ in PHASES:
                if name.startswith("ffn"):
                    ffn(int(name[3:]))
                elif name != "final":
                    {"mem": mem, "mixa": mixa, "mixb": mixb, "ssd": ssd}[name]()
            for c in range(4):
                if c % 2:
                    sp.wait_ge(act_done, act_.at(f"out {c}"))
                else:
                    sp.wait_ge(vec_done, vec.at(f"out {c}"))
                tt, f = c // 2, slice(512 * (c % 2), 512 * (c % 2) + 512)
                sp.dma_start(out[0][tt * P:tt * P + P, f], yout[:, tt, f]).then_inc(stored, 16)
            sp.wait_ge(stored, 64)

        @block.gpsimd
        def _(pool):
            pool.memset(rows[:, :, :], 0.0).then_inc(pool_done, pool_("rows 0"))
            pool.memset(ones[:, :], 1.0).then_inc(pool_done, pool_("ones"))
            pool.memset(ident[:, :], 0.0).then_inc(pool_done, pool_("ident 0"))
            pool.wait_ge(pool_done, pool_.at("ident 0"))
            pool.affine_select(out=ident[:, :], in_=ident[:, :], compare_op=ALU.not_equal, fill=1.0, base=0,
                               pattern=[[-1, P]], channel_multiplier=1).then_inc(pool_done, pool_("ident"))

            def fill(dst, name, steps):
                pool.memset(dst, 0.0).then_inc(pool_done, pool_(name + " 0"))
                for j, (view, value, base, pattern, compare) in enumerate(steps):
                    pool.wait_ge(pool_done, pool_.at(f"{name} {j}"))
                    pool.affine_select(out=view, in_=view, compare_op=compare, fill=value, base=base, pattern=pattern,
                                       channel_multiplier=-pattern[0][0] // abs(pattern[0][0])).then_inc(pool_done, pool_(f"{name} {j + 1}"))

            eye = [[-1, P]]
            fill(mask[:, :], "mask", [(mask[:, 0:P], 1.0, 0, eye, ALU.is_gt), (mask[:, P:2 * P], 1.0, -P, eye, ALU.is_gt),
                                      (mask[:, 2 * P:], 1.0, 0, eye, ALU.is_gt)])
            fill(window[:, :], "window", [(window[:, 0:P], NEG, 0, eye, ALU.is_ge),
                                          (window[:, 2 * P:], NEG, 0, eye, ALU.is_ge),
                                          (window[:, P:2 * P], NEG, 0, [[1, P]], ALU.is_gt)])
            fill(rotate[:, :], "rotate", [s for j in (0, B_HD) for s in (
                (rotate[:, j:j + 8], -1.0, -j - 8, [[-1, 8]], ALU.not_equal),
                (rotate[:, j + 8:j + 16], 1.0, -j, [[-1, 8]], ALU.not_equal))])
            fill(swap[:, :], "swap", [(swap[:, 0:64], 1.0, -64, [[-1, 64]], ALU.not_equal),
                                      (swap[:, 64:P], 1.0, 0, [[-1, 64]], ALU.not_equal)])
            def mixa():
                for h in range(4):
                    pool.wait_ge(act_done, act_.at(f"A e {h}"))
                    for j, o in enumerate((0, 2 * P)):
                        blk = a_e[:, h, o:o + P]
                        pool.affine_select(out=blk, in_=blk, compare_op=ALU.is_ge, fill=0.0, base=0, pattern=[[1, P]],
                                           channel_multiplier=-1).then_inc(pool_done, pool_(f"A e {h} {j}"))
                for j in range(4):
                    pool.wait_ge(act_done, act_.at(f"A tanh {j}"))
                    og = a_o[:, 2 * j:2 * j + 2]
                    pool.tensor_scalar(og, og, 0.5, 0.5, ALU.mult, ALU.add).then_inc(pool_done, pool_(f"A gate {j}"))

            def mixb():
                for j, (t0, n) in enumerate(B_STEPS):
                    xt = b_x[:, t0:t0 + n]
                    pool.wait_ge(pe_done, pe_.at(f"B rot {j}"))
                    pool.tensor_tensor(xt, xt, wide(rope[:, 0, :], n), ALU.mult).then_inc(pool_done, pool_(f"B cos {j}"))
                    pool.wait_ge(vec_done, vec.at(f"B sin {j}"))
                    pool.wait_ge(pool_done, pool_.at(f"B cos {j}"))
                    pool.tensor_tensor(xt, xt, tiles(b_rot[:, j % 2])[:, 0:n], ALU.add).then_inc(pool_done, pool_(f"B x {j}"))

            def norm(n):
                pool.wait_ge(squared, 4 * n + 2)
                for c in range(1, 4):
                    if c > 1:
                        pool.wait_ge(squared, 4 * n + c + 1)
                        pool.wait_ge(sq_summed, 3 * n + c - 1)
                    pool.tensor_tensor(sq[:, 0], sq[:, 0], sq[:, c], ALU.add).then_inc(sq_summed, 1)

            def weigh(j):
                for h in range(4 * j, 4 * j + 4):
                    pool.wait_ge(act_done, act_.at(f"S e {h}"))
                    pool.wait_ge(vec_done, vec.at(f"S CB {h // 8}"))
                    pool.tensor_tensor(s_e[:, h % 6], s_e[:, h % 6], s_cb[:, h // 8], ALU.mult).then_inc(pool_done, pool_(f"S s {h}"))

            def gate(c):
                q, t0 = 2 * (c % 2), conv_tile(c)
                pool.wait_ge(act_done, act_.at(f"S th {c}"))
                pool.tensor_scalar(s_in[:, q:q + 2], s_in[:, q:q + 2], 1.0, None, ALU.add).then_inc(pool_done, pool_(f"S th {c}"))
                pool.wait_ge(pool_done, pool_.at(f"S th {c}"))
                pool.tensor_tensor(s_x[:, t0:t0 + 2], s_in[:, q:q + 2], s_cv[:, q:q + 2], ALU.mult).then_inc(pool_done, pool_(f"S x {c}"))

            def ssd():
                def squares(i):
                    pool.wait_ge(act_done, act_.at(f"S zsq {i}"))
                    if i > 1:
                        pool.wait_ge(pe_done, pe_.at(f"S zsum {i - 2}"))
                    z = s_z[:, 2 * (i % 2):2 * (i % 2) + 2]
                    pool.tensor_tensor(s_zsq[:, i % 2], z[:, 0], z[:, 1], ALU.add).then_inc(pool_done, pool_(f"S zsq {i}"))

                for c in range(21):
                    if 9 <= c < 17:
                        weigh(c - 9)
                    if c < 12:
                        gate(c)
                    if c > 12:
                        squares(c - 13)

            for name, _, _ in PHASES[:-1]:
                norm(norm_of[name][0])
                if name in ("mixa", "mixb", "ssd"):
                    {"mixa": mixa, "mixb": mixb, "ssd": ssd}[name]()

        @block.scalar
        def _(act):
            roots = [0]

            def round_(u, i=0):
                if isinstance(i, int) and u + 6 * i >= NU:
                    return
                act.wait_ge(w_landed[u % RING], 16 * (u // RING + 1) + 32 * i)
                if u >= RING:
                    act.wait_ge(w_used, u - RING + 1 + 6 * i)
                act.activation(w_hi[:, u % RING, :], w_raw[:, u % RING, :], ACT.Copy).then_inc(w_rounded, 1)

            def evacuated(u, i=0):
                act.wait_ge(drained[u % RING], fills[u] + 2 * i)

            def norm(n, gain, split=True):
                src = x if n else mem_t

                def squares():
                    for c in range(4):
                        act.activation(sq[:, c], src[:, 2 * c:2 * c + 2], ACT.Square).then_inc(squared, 1)

                if n == 1:
                    act.wait_ge(stat_done, 1)
                    act.wait_ge(x_new, 8)
                    squares()
                    act.wait_ge(w_used, U["ffn0"])
                for c in range(4):
                    act.wait_ge(x_new, 4 * n + c + 1)
                    if split:
                        for k in (2 * c, 2 * c + 1):
                            act.activation(xg_hi[:, k], src[:, k], ACT.Identity, scale=col(gain, k)).then_inc(xh_ready, 1)
                if n == 0:
                    round_(1)
                if n != 1:
                    squares()

            def root(y, v):
                k = roots[0]
                roots[0] += 1
                act.preload_act_table_set(SETS["lnexp"])
                act.wait_ge(rs_vec, 4 * k + 1)
                act.activation(y, v, ACT.Ln).then_inc(rs_act, 1)
                act.wait_ge(rs_act, 2 * k + 1)
                act.activation(y, y, ACT.Exp, scale=-0.5).then_inc(rs_act, 1)

            def ffn(f, n, gain):
                u = U[f"ffn{f}"]
                norm(n, gain)
                round_(u + 2)
                round_(u + 3)
                if f == 0:
                    for j in range(2):
                        act.wait_ge(pe_done, pe_.at("M v"))
                        act.activation(mem_v[:, j], ps[:, 2 + j, :], ACT.Copy).then_inc(act_done, act_(f"M v {j}"))
                root(rs_y[:, :], rs_v[:, :])
                act.preload_act_table_set(SETS["silu"])

                def silu(v, i, it=0):
                    evacuated(v, it)
                    act.activation(gate_s, gate_s, ACT.Silu).then_inc(ffn_silu, 1)

                def product(i, p):
                    act.wait_ge(ffn_h, NI * nth[f] + i + 1)
                    act.activation(y_hi[:, 2 * p:2 * p + 2], tiles(up_s), ACT.Copy).then_inc(ffn_hh, 1)

                def step(g, i, p, it=0):
                    round_(g + 2, it)
                    silu(g, i, it)
                    round_(g + 3, it)
                    product(i, p)
                    round_(g + 4, it)

                silu(u, 0)
                product(0, 0)
                step(u + 2, 1, 1)
                if f == 0:
                    root(KB(48, 4), KB(44, 4))
                    act.preload_act_table_set(SETS["silu"])
                step(u + 5, 2, 0)
                if f == 1:
                    act.wait_ge(vec_done, vec.at("sine 0"))
                    for j in range(2):
                        act.activation(rope[:, j], rope[:, j], ACT.Sin).then_inc(act_done, act_(f"rope {j}"))
                bodies = (NI - 3) // 2
                peel = f"ffn{f}" == LAST
                with act.Fori(0, bodies - peel) as b:
                    step(u + 8, 2 * b + 3, 1, b)
                    step(u + 11, 2 * b + 4, 0, b)
                if peel:
                    step(u + 8 + 6 * (bodies - 1), NI - 2, 1)
                    step(u + 11 + 6 * (bodies - 1), NI - 1, 0)
                round_(u + 3 * NI + 1)

            def mem(n, gain):
                u = U["mem"]
                norm(n, gain)
                round_(u + 2)
                round_(u + 3)
                root(rs_y[:, :], rs_v[:, :])
                round_(u + 4)
                for j in range(2):
                    evacuated(u + j)
                    act.activation(tiles(KB(40 + 2 * j, 2)), mem_k[:, 2 * j:2 * j + 2],
                                   ACT.Square).then_inc(act_done, act_(f"M sq {j}"))
                round_(u + 5)

            def query_squares(tag, u, xq, xsq, layer):
                for j in range(2):
                    evacuated(u + j)
                    q = xq[:, 2 * j:2 * j + 2]
                    act.activation(xsq[:, 2 * j:2 * j + 2], q, ACT.Square).then_inc(act_done, act_(f"{tag} xsq {j}"))
                    act.activation(q, q, ACT.Identity, scale=gain_qk[:, layer:layer + 1]).then_inc(act_done, act_(f"{tag} xq {j}"))

            def mem_exps(tag, p):
                act.wait_ge(vec_done, vec.at(f"{tag} m -max"))
                for h in range(4):
                    for tt in range(2):
                        c = 2 * h + tt
                        act.activation(p[:, c], ps[:, h, tt * T:tt * T + T], ACT.Exp, scale=m_r[:, c:c + 1], bias=m_stat[:, c:c + 1],
                                       accum_out=m_sum[:, c:c + 1]).then_inc(act_done, act_(f"{tag} m exp {c}"))

            def mem_turned(tag, pt, base):
                for h in range(4):
                    act.wait_ge(pe_done, pe_.at(f"{tag} m pT {h}"))
                    act.activation(pt[:, 2 * h:2 * h + 2], tiles(ps[:, base + h, :]),
                                   ACT.Copy).then_inc(act_done, act_(f"{tag} m pT {h}"))

            def mem_high(tag, base):
                act.wait_ge(pe_done, pe_.at(f"{tag} m o"))
                act.activation(y_hi[:, 8:12], tiles(ps[:, base:base + 2, :].rearrange("p a b -> p (a b)")),
                               ACT.Copy).then_inc(act_done, act_(f"{tag} m hi"))

            def mixa(n, gain):
                u, v = U["mixa"], U["mixa_out"]
                norm(n, gain)
                round_(u + 2)
                round_(u + 3)
                root(rs_y[:, :], rs_v[:, :])
                round_(u + 4)
                g = a_rows[0:4]
                act.wait_ge(vec_done, vec.at("A -abs"))
                act.activation(g[:, GL], g[:, GL], ACT.Exp).then_inc(act_done, act_("A exp"))
                act.wait_ge(act_done, act_.at("A exp"))
                act.activation(g[:, GL], g[:, GL], ACT.Ln, bias=ones[0:4, 0:1]).then_inc(act_done, act_("A softplus"))
                round_(u + 5)
                act.wait_ge(vec_done, vec.at("A em"))
                act.activation(g[:, GE], g[:, GE], ACT.Exp, scale=-1.0).then_inc(act_done, act_("A em"))
                round_(u + 6)
                round_(u + 7)
                act.wait_ge(vec_done, vec.at("A u_col"))
                act.wait_ge(pe_done, pe_.at("A -m"))
                for h in range(4):
                    nm = ps[:, h // 2, (h % 2) * T:(h % 2) * T + T]
                    act.activation(a_e[:, h, 0:T], nm, ACT.Exp, bias=u_col[:, h:h + 1]).then_inc(act_done, act_(f"A e0 {h}"))
                    act.activation(a_e[:, h, T:], nm[:, P:], ACT.Exp, bias=u_col[:, 4 + h:5 + h]).then_inc(act_done, act_(f"A e {h}"))
                round_(u + 8)
                round_(u + 9)
                round_(u + 10)
                for j in range(2):
                    act.wait_ge(pe_done, pe_.at(f"A rden {j}"))
                    act.activation(a_rden[:, 2 * j:2 * j + 2], tiles(ps[:, STAT, :]), ACT.Copy).then_inc(act_done, act_(f"A rden {j}"))
                    round_(u + 11 + j)
                for j in range(4):
                    act.wait_ge(pe_done, pe_.at("A v"))
                    act.activation(a_v[:, j // 2, (j % 2) * 512:(j % 2) * 512 + 512], ps[:, j, :],
                                   ACT.Copy).then_inc(act_done, act_(f"A v {j}"))
                round_(u + 13)
                query_squares("A", u + 9, xq_a, xsq_a, 0)
                act.wait_ge(pe_done, pe_.at("A num 3"))
                for h in range(4):
                    act.wait_ge(vec_done, vec.at(f"A h {h}"))
                    act.activation(a_hsq[:, 2 * h:2 * h + 2], a_h[:, 2 * h:2 * h + 2],
                                   ACT.Square).then_inc(act_done, act_(f"A hsq {h}"))
                round_(u + 14)
                root(m_r, m_v)
                root(KB(28, 4), KB(24, 4))
                act.preload_act_table_set(SETS["exp"])
                round_(u + 15)

                def tanh(j):
                    evacuated(u + 11 + j)
                    act.activation(a_o[:, 2 * j:2 * j + 2], a_o[:, 2 * j:2 * j + 2], ACT.Tanh,
                                   scale=0.5).then_inc(act_done, act_(f"A tanh {j}"))

                def high(j):
                    act.wait_ge(vec_done, vec.at(f"A y {j}"))
                    act.activation(y_hi[:, 2 * j:2 * j + 2], a_h[:, 2 * j:2 * j + 2], ACT.Copy).then_inc(act_done, act_(f"A hi {j}"))

                tanh(0)
                tanh(1)
                mem_exps("A", p_a)
                high(0)
                high(1)
                round_(u + 16)
                tanh(2)
                high(2)
                round_(v + 2)
                tanh(3)
                high(3)
                mem_turned("A", pt_a, 4)
                round_(v + 3)
                mem_high("A", 4)
                for j in range(4, 8):
                    round_(v + j)

            def mixb(n, gain):
                u, v = U["mixb"], U["mixb_out"]
                norm(n, gain)
                round_(u + 2)
                round_(u + 3)
                root(rs_y[:, :], rs_v[:, :])

                def square(j):
                    t0, w = B_STEPS[j]
                    q = b_x[:, t0:t0 + w]
                    evacuated(u + 2 + j)
                    act.activation(tiles(b_sq[:, j - 1] if j else b_sqk), q, ACT.Square).then_inc(act_done, act_(f"B sq {j}"))
                    if j:
                        act.activation(q, q, ACT.Identity, scale=gain_b[:, 0:1]).then_inc(act_done, act_(f"B n {j}"))

                round_(u + 4)
                query_squares("B", u, xq_b, xsq_b, 1)
                round_(u + 5)
                square(0)
                root(m_r, m_v)
                round_(u + 6)
                root(b_ry, b_rv)
                mem_exps("B", p_b)
                square(1)
                round_(v)
                mem_turned("B", pt_b, 0)
                square(2)
                act.wait_ge(pe_done, pe_.at("B k v"))
                act.activation(b_v[:, :], tiles(ps[:, STAT, 0:T], P), ACT.Copy).then_inc(act_done, act_("B v"))
                act.activation(b_kx, ps[:, STAT, T:], ACT.Copy).then_inc(act_done, act_("B kx"))
                round_(v + 1)
                mem_high("B", 0)
                square(3)
                round_(v + 2)
                square(4)
                root(b_r[:, :, :].rearrange("p a b -> p (a b)"), b_rvt[:, 0:32])

                def exps(b):
                    act.wait_ge(vec_done, vec.at(f"B sink {b}"))
                    for h in range(4 * b, 4 * b + 4):
                        for blk, (lo, hi) in enumerate(BLOCKS):
                            s = b_s[:, h % 8, lo:hi]
                            act.activation(s, s, ACT.Exp, scale=b_r[:, blk, h:h + 1], bias=b_stat[:, 1, h, blk:blk + 1],
                                           accum_out=b_stat[:, 2, h, blk:blk + 1]).then_inc(act_done, act_(f"B exp {h} {blk}"))
                    st = b_stat[:, 3, 4 * b:4 * b + 4]
                    act.activation(st, st, ACT.Exp).then_inc(act_done, act_(f"B sink {b}"))

                def turned(b):
                    for h in range(4 * b, 4 * b + 4):
                        act.wait_ge(pe_done, pe_.at(f"B pT {h}"))
                        act.activation(b_pt[:, h % 4], ps[:, BANK["T", h], 0:384], ACT.Copy).then_inc(act_done, act_(f"B pT {h}"))

                def high(b):
                    act.wait_ge(pe_done, pe_.at(f"B o {b}"))
                    act.activation(y_hi[:, 2 * b:2 * b + 2], tiles(ps[:, STAT, :]), ACT.Copy).then_inc(act_done, act_(f"B hi {b}"))

                exps(0)
                turned(0)
                exps(1)
                high(0)
                round_(v + 3)
                round_(v + 4)
                turned(1)
                high(1)
                exps(2)
                round_(v + 5)
                turned(2)
                high(2)
                exps(3)
                round_(v + 6)
                turned(3)
                high(3)
                round_(v + 7)

            def ssd(n, gain):
                norm(n, gain)
                u = U["dt"]
                round_(u + 2)
                round_(u + 3)
                root(rs_y[:, :], rs_v[:, :])
                round_(u + 4)
                act.activation(a_log, a_log, ACT.Exp).then_inc(act_done, act_("S a"))
                act.wait_ge(vec_done, vec.at("S -abs"))
                act.activation(s_dtl, s_dtl, ACT.Exp).then_inc(act_done, act_("S dt exp"))
                act.wait_ge(act_done, act_.at("S dt exp"))
                act.activation(s_dtl, s_dtl, ACT.Ln, bias=ones[0:32, 0:1]).then_inc(act_done, act_("S softplus"))
                act.preload_act_table_set(SETS["exp"])

                def tap(c):
                    q = 2 * (c % 2)
                    evacuated(U["bc"] + c)
                    for t in range(2):
                        if c > 1:
                            act.wait_ge(pool_done, pool_.at(f"S x {c - 2}"))
                        act.activation(s_cv[:, q + t], s_in[:, q + t], ACT.Identity, scale=col("conv_w3", conv_tile(c) + t),
                                       bias=col("conv_b", conv_tile(c) + t)).then_inc(act_done, act_(f"S tap {c} {t}"))

                def tanh(c):
                    q = 2 * (c % 2)
                    act.wait_ge(vec_done, vec.at(f"S tap0 {c} 1"))
                    act.activation(s_in[:, q:q + 2], s_cv[:, q:q + 2], ACT.Tanh, scale=0.5).then_inc(act_done, act_(f"S th {c}"))

                def exps(j):
                    for h in range(4 * j, 4 * j + 4):
                        if h % 2 == 0:
                            act.wait_ge(vec_done, vec.at(f"S seg {h + 1} 2"))
                            for i in (h, h + 1):
                                act.activation(s_e[:, i % 6, P:2 * P], half(i % 4 // 2, i)[:, P:], ACT.Exp,
                                               bias=bias_col[:, 64 + i:65 + i]).then_inc(act_done, act_(f"S e {i} 1"))
                        e = blocks02(h)
                        act.activation(e, e, ACT.Exp).then_inc(act_done, act_(f"S e {h}"))

                for c in range(28):
                    if c > 1:
                        round_(U["bc"] + c + 2)
                    if 2 <= c < 14:
                        tanh(c - 2)
                    if 1 <= c < 13:
                        tap(c - 1)
                    if 9 <= c < 17:
                        exps(c - 9)
                    if 13 <= c < 21:
                        i = c - 13
                        q = slice(2 * (i % 2), 2 * (i % 2) + 2)
                        evacuated(U["z"] + i)
                        act.activation(s_zth[:, q], s_z[:, q], ACT.Tanh, scale=0.5).then_inc(act_done, act_(f"S zth {i}"))
                        z_square(i)
                    if 21 <= c < 25:
                        branch_gate(s_gate[:, c - 21], "ga", c - 21)
                    if c in (19, 23):
                        root(g_y, g_v)
                        act.preload_act_table_set(SETS["exp"])
                    if c == 21:
                        high(range(0, 8))
                    if c == 24:
                        high(range(8, 12))
                    if c >= 25:
                        branch_gate(s_gate_b[c - 25], "gb", c - 25)
                    if c == 25:
                        high(range(12, 16))
                for j in range(8):
                    round_(U["aproj"] + j + 2)
                    if j == 0:
                        branch_gate(s_gate_b[3], "gb", 3)
                u = U["sconv"]

                def conv_high(j):
                    act.wait_ge(vec_done, vec.at(f"S sy {j}"))
                    act.activation(y_hi[:, 2 * j:2 * j + 2], tiles(sc_b[:, j % 2]), ACT.Copy).then_inc(act_done, act_(f"S shi {j}"))

                for j in range(4):
                    k, q = u + 3 * j, j % 2
                    round_(k + 2)
                    if j:
                        conv_high(j - 1)
                    round_(k + 3)
                    round_(k + 4)
                    evacuated(k + 1)
                    for t in range(2):
                        act.activation(tiles(sc_v[:, q])[:, t], tiles(sc_prod[:, q])[:, t], ACT.Identity,
                                       scale=col("sconv_w2", 2 * j + t)).then_inc(act_done, act_(f"S stap {j} {t}"))
                conv_high(3)
                for j in range(4):
                    round_(U["sproj"] + j + 2)
                    act.wait_ge(vec_done, vec.at(f"S merged {j}"))
                    act.activation(xg_hi[:, 2 * j:2 * j + 2], s_merged[:, 2 * j:2 * j + 2], ACT.Copy).then_inc(act_done, act_(f"S mhi {j}"))
                for j in range(4):
                    round_(U["w_o"] + j + 2)

            def branch_gate(g, name, j):
                evacuated(U[name] + j)
                act.activation(g, g, ACT.Tanh, scale=0.5).then_inc(act_done, act_(f"S {name} {j}"))

            def z_square(i):
                z = s_z[:, 2 * (i % 2):2 * (i % 2) + 2]
                act.wait_ge(vec_done, vec.at(f"S yz {i}"))
                act.activation(z, s_x[:, 2 * i:2 * i + 2], ACT.Square).then_inc(act_done, act_(f"S zsq {i}"))

            def high(ks):
                for k in ks:
                    act.wait_ge(vec_done, vec.at(f"S yn {k}"))
                    act.activation(y_hi[:, k], s_x[:, k], ACT.Copy).then_inc(act_done, act_(f"S hi {k}"))

            round_(0)
            for name, gain, _ in PHASES:
                n = norm_of[name][0]
                if name.startswith("ffn"):
                    ffn(int(name[3:]), n, gain)
                elif name != "final":
                    {"mem": mem, "mixa": mixa, "mixb": mixb, "ssd": ssd}[name](n, gain)
            norm(norm_of["final"][0], "final", split=False)
            root(fin_r, fin_v)
            for c in (1, 3):
                act.wait_ge(rs_vec, 4 * roots[0])
                act.wait_ge(pe_done, pe_.at("out"))
                act.activation(yout[:, c // 2, 512:], ps[:, c, :], ACT.Identity, scale=fin_r[:, c // 2:c // 2 + 1]).then_inc(act_done, act_(f"out {c}"))

        @block.vector
        def _(dve):
            roots = [0]

            def split(u, i=0):
                if isinstance(i, int) and u + 6 * i >= NU:
                    return
                s = u % RING
                dve.wait_ge(w_rounded, u + 1 + 6 * i)
                dve.tensor_tensor(w_lo[:, s, :], w_raw[:, s, :], w_hi[:, s, :].bitcast(F32),
                                  ALU.subtract).then_inc(w_split, 1)

            def norm(n, gain, factor, before=None, split_x=True):
                src = x if n else mem_t

                def low(c):
                    for k in (2 * c, 2 * c + 1):
                        dve.wait_ge(xh_ready, 8 * n + k + 1)
                        dve.scalar_tensor_tensor(out=xg_lo[:, k], in0=src[:, k], scalar=col(gain, k),
                                                 in1=xg_hi[:, k].bitcast(F32), op0=ALU.mult,
                                                 op1=ALU.subtract).then_inc(xl_ready, 1)
                if n == 1:
                    for c in range(4):
                        low(c)
                    return
                for c in range(4):
                    xc = src[:, 2 * c:2 * c + 2]
                    if c < 3:
                        dve.wait_ge(acc_ready, 3 * n + c + 1)
                    elif factor is None:
                        dve.wait_ge(turned, n + 1)
                    else:
                        dve.wait_ge(w_used, before + 1)
                    if factor is None:
                        dve.tensor_copy(xc, tiles(ps[:, c, :])).then_inc(x_new, 1)
                    else:
                        dve.scalar_tensor_tensor(out=xc, in0=tiles(ps[:, c, :]), scalar=factor, in1=xc,
                                                 op0=ALU.mult, op1=ALU.add).then_inc(x_new, 1)
                    if split_x and c and n:
                        low(c - 1)
                if n == 0:
                    split(0)
                    low(0)
                    low(1)
                    low(2)
                if split_x:
                    low(3)
                if n == 0:
                    split(1)

            def root(*args, **kw):
                for _ in root_steps(*args, **kw):
                    pass

            def root_steps(result, stat, v, y, t, scale, eps=EPS, name=None):
                k = roots[0]
                roots[0] += 1
                if name:
                    root_.found[name] = 4 * k + 1
                dve.tensor_scalar(v, stat, scale, eps, ALU.mult, ALU.add).then_inc(rs_vec, 1)
                yield
                dve.wait_ge(rs_act, 2 * k + 2)
                dve.tensor_tensor(t, y, y, ALU.mult).then_inc(rs_vec, 1)
                yield
                dve.wait_ge(rs_vec, 4 * k + 2)
                dve.scalar_tensor_tensor(out=t, in0=t, scalar=-0.5, in1=v, op0=ALU.mult,
                                         op1=ALU.mult).then_inc(rs_vec, 1)
                yield
                dve.wait_ge(rs_vec, 4 * k + 3)
                dve.scalar_tensor_tensor(out=result, in0=t, scalar=1.5, in1=y, op0=ALU.add,
                                         op1=ALU.mult).then_inc(rs_vec, 1)
                dve.wait_ge(rs_vec, 4 * k + 4)

            def token_root(n):
                dve.wait_ge(stat_done, n + 1)
                root(rstd[:, :], ps[:, STAT, 0:T], rs_v[:, :], rs_y[:, :], rs_t[:, :], 1.0 / D)

            def evac(dst, u, i=0, scale=1.0, r=None):
                dve.wait_ge(w_used, u + 1 + 6 * i)
                dve.scalar_tensor_tensor(out=dst, in0=tiles(ps[:, bank(u), :]), scalar=scale, in1=wide(rstd[:, :] if r is None else r),
                                         op0=ALU.mult, op1=ALU.mult).then_inc(drained[u % RING], 1)

            def ffn(f, n, gain, factor):
                u = U[f"ffn{f}"]
                norm(n, gain, factor, u - 1)
                if f == 0:
                    evac(tiles(KB(34, 2)), u - 1)
                split(u + 2)
                split(u + 3)
                token_root(n)

                def product(g, i, it=0):
                    evac(tiles(up_s), g + 1, it)
                    dve.wait_ge(drained[(g + 1) % RING], fills[g + 1] + 2 * it)
                    dve.wait_ge(ffn_silu, NI * nth[f] + i + 1)
                    dve.tensor_tensor(up_s, up_s, gate_s, ALU.mult).then_inc(ffn_h, 1)

                def low(i, p):
                    dve.wait_ge(ffn_hh, NI * nth[f] + i + 1)
                    dve.tensor_tensor(y_lo[:, 2 * p:2 * p + 2], tiles(up_s), y_hi[:, 2 * p:2 * p + 2].bitcast(F32),
                                      ALU.subtract).then_inc(ffn_hl, 1)

                extra = iter(()) if f > 1 else rope_angles() if f else mem_keys()

                def step(g, i, p, it=0, more=False):
                    split(g + 2, it)
                    if more:
                        next(extra, None)
                    evac(tiles(gate_s), g, it)
                    split(g + 3, it)
                    if more:
                        next(extra, None)
                    product(g, i, it)
                    low(i, p)
                    split(g + 4, it)
                    if more:
                        next(extra, None)

                evac(tiles(gate_s), u)
                product(u, 0)
                low(0, 0)
                step(u + 2, 1, 1, more=f == 1)
                if f == 0:
                    next(extra)
                    gains()
                step(u + 5, 2, 0, more=True)
                for _ in extra:
                    pass
                bodies = (NI - 3) // 2
                peel = f"ffn{f}" == LAST
                with dve.Fori(0, bodies - peel) as b:
                    step(u + 8, 2 * b + 3, 1, b)
                    step(u + 11, 2 * b + 4, 0, b)
                if peel:
                    step(u + 8 + 6 * (bodies - 1), NI - 2, 1)
                    step(u + 11 + 6 * (bodies - 1), NI - 1, 0)
                split(u + 3 * NI + 1)

            def mem(n, gain, factor):
                u = U["mem"]
                norm(n, gain, factor, u - 1)
                split(u + 2)
                split(u + 3)
                dve.wait_ge(pe_done, pe_.at("vectors"))
                dve.tensor_copy(cols[:, 0, 8:], ps[:, 3, 8:P]).then_inc(vec_done, vec("cols 0"))
                dve.tensor_copy(cols[:, 1:, :], ps[:, 3, P:3 * P].rearrange("p (a b) -> p a b", a=2)).then_inc(vec_done, vec("cols"))
                token_root(n)
                evac(mem_k[:, 0:2], u)
                evac(mem_k[:, 2:4], u + 1)
                split(u + 4)
                for c in range(4):
                    if c < 3:
                        dve.wait_ge(acc_ready, 4 + c)
                    else:
                        dve.wait_ge(turned, 2)
                    dve.tensor_copy(x[:, 2 * c:2 * c + 2], tiles(ps[:, c, :])).then_inc(x_new, 1)
                evac(tiles(KB(32, 2)), u + 2)
                split(u + 5)
                dve.wait_ge(pe_done, pe_.at("M ksum"))
                dve.tensor_copy(KB(44, 4), ps[:, 0:2, :].rearrange("p a b -> p (a b)")).then_inc(vec_done, vec("M ksum"))

            def mem_keys():
                r = KB(48, 4)
                dve.wait_ge(vec_done, vec.at("M ksum"))
                yield from root_steps(r, KB(44, 4), KB(44, 4), r, KB(52, 4), 1.0 / M_HD)
                dve.tensor_tensor(mem_k[:, :], mem_k[:, :], tiles(r), ALU.mult).then_inc(vec_done, vec("mem_k"))

            def gains():
                for l in range(2):
                    dve.scalar_tensor_tensor(out=gain_qk[:, l:l + 1], in0=col(f"xa_q{l}"), scalar=M_HD ** -0.5,
                                             in1=col(f"xa_k{l}"), op0=ALU.mult, op1=ALU.mult).then_inc(vec_done, vec(f"gain_qk {l}"))
                dve.tensor_scalar(gain_b[:, 0:1], col("b_q"), B_HD ** -0.5, None, ALU.mult).then_inc(vec_done, vec("gain_b"))
                ang = rope[:, 0]
                dve.tensor_copy(ang, pos).then_inc(vec_done, vec("pos"))
                dve.wait_ge(vec_done, vec.at("pos"))
                dve.tensor_scalar(ang, ang, inv_freq[:, 0:1], None, ALU.mult).then_inc(vec_done, vec("angle"))

            def rope_angles():
                ang, turns, whole = rope[:, 0], KB(37, 1), KB(38, 1)
                whole_i = whole.bitcast(I32)
                two_pi = 2 * np.pi
                c1 = 6.28125
                c2 = float(np.float32(np.round((two_pi - c1) * 2.0 ** 21) / 2.0 ** 21))
                c3 = two_pi - c1 - c2
                for j, shift in ((1, 0.0), (0, 0.25)):
                    dve.wait_ge(vec_done, vec.at("angle"))
                    if j == 0:
                        dve.wait_ge(vec_done, vec.at("sine 1"))
                    dve.tensor_scalar(turns, ang, 1 / two_pi, shift, ALU.mult, ALU.add).then_inc(vec_done, vec(f"turns {j}"))
                    dve.wait_ge(vec_done, vec.at(f"turns {j}"))
                    dve.tensor_copy(whole_i, turns).then_inc(vec_done, vec(f"whole {j}"))
                    yield
                    dve.wait_ge(vec_done, vec.at(f"whole {j}"))
                    dve.tensor_copy(turns, whole_i).then_inc(vec_done, vec(f"whole turns {j}"))
                    dve.wait_ge(vec_done, vec.at(f"whole turns {j}"))
                    src = ang
                    for k, c in enumerate((c1, c2, c3)):
                        dve.scalar_tensor_tensor(out=rope[:, j], in0=turns, scalar=-c, in1=src, op0=ALU.mult,
                                                 op1=ALU.add).then_inc(vec_done, vec(f"reduced {j} {k}"))
                        dve.wait_ge(vec_done, vec.at(f"reduced {j} {k}"))
                        src = rope[:, j]
                    yield
                    dve.tensor_scalar(rope[:, j], rope[:, j], shift * two_pi, np.pi - 1e-6, ALU.add, ALU.min).then_inc(vec_done, vec(f"shifted {j}"))
                    dve.wait_ge(vec_done, vec.at(f"shifted {j}"))
                    dve.tensor_scalar(rope[:, j], rope[:, j], 1e-6 - np.pi, None, ALU.max).then_inc(vec_done, vec(f"sine {j}"))
                    yield

            def query_root(tag):
                dve.wait_ge(pe_done, pe_.at(f"{tag} xsum"))
                root(m_r, ps[:, STAT, 0:8], m_v, m_r, m_t, 1.0 / M_HD)

            def mem_max(tag):
                for h in range(4):
                    dve.wait_ge(pe_done, pe_.at(f"{tag} m s {h}"))
                    dve.tensor_reduce(m_stat[:, 2 * h:2 * h + 2], tiles(ps[:, h, :]), AXX, ALU.max).then_inc(vec_done, vec(f"{tag} m max {h}"))
                dve.wait_ge(vec_done, vec.at(f"{tag} m max 3"))
                dve.scalar_tensor_tensor(out=m_stat, in0=m_stat, scalar=-1.0, in1=m_r, op0=ALU.mult,
                                         op1=ALU.mult).then_inc(vec_done, vec(f"{tag} m -max"))

            def mem_probs(tag, p):
                dve.wait_ge(act_done, act_.at(f"{tag} m exp 7"))
                dve.reciprocal(m_inv, m_sum).then_inc(vec_done, vec(f"{tag} m inv"))
                dve.wait_ge(vec_done, vec.at(f"{tag} m inv"))
                for c in range(8):
                    dve.tensor_scalar(p[:, c], p[:, c], m_inv[:, c:c + 1], None, ALU.mult).then_inc(vec_done, vec(f"{tag} m p {c}"))

            def mem_low(tag, base):
                dve.wait_ge(act_done, act_.at(f"{tag} m hi"))
                dve.tensor_tensor(y_lo[:, 8:12], tiles(ps[:, base:base + 2, :].rearrange("p a b -> p (a b)")), y_hi[:, 8:12].bitcast(F32),
                                  ALU.subtract).then_inc(vec_done, vec(f"{tag} m lo"))

            def mixa(n, gain, factor):
                u, v = U["mixa"], U["mixa_out"]
                norm(n, gain, factor, u - 1)
                split(u + 2)
                split(u + 3)
                token_root(n)
                g = a_rows[0:4]
                dve.wait_ge(w_used, u + 1)
                dve.tensor_tensor(g[:, GI:GF + 1], tiles(ps[0:4, bank(u), :]), wide(rstd[0:4, :]), ALU.mult).then_inc(drained[u % RING], 1)
                evac(a_q[:, 0:2], u + 1, scale=A_HD ** -0.5)
                split(u + 4)
                dve.wait_ge(drained[u % RING], fills[u])
                for j, name in ((GI, "A i"), (GF, "A f")):
                    dve.tensor_scalar(g[:, j], g[:, j], gate_bias[:, j:j + 1], None, ALU.add).then_inc(vec_done, vec(name))
                dve.wait_ge(vec_done, vec.at("A f"))
                dve.scalar_tensor_tensor(out=g[:, GL], in0=g[:, GF], scalar=-1.0, in1=g[:, GF], op0=ALU.mult,
                                         op1=ALU.min).then_inc(vec_done, vec("A -abs"))
                evac(a_q[:, 2:4], u + 2, scale=A_HD ** -0.5)
                split(u + 5)
                dve.wait_ge(act_done, act_.at("A softplus"))
                dve.scalar_tensor_tensor(out=g[:, LOGF], in0=g[:, GF], scalar=0.0, in1=g[:, GL], op0=ALU.min,
                                         op1=ALU.subtract).then_inc(vec_done, vec("A logf"))
                dve.wait_ge(vec_done, vec.at("A logf"))
                one = ones[0:4, 0:1].broadcast_to([4, T])
                dve.tensor_tensor_scan(g[:, CUM], one, g[:, LOGF], 0.0, ALU.mult, ALU.add).then_inc(vec_done, vec("A cum"))
                dve.wait_ge(vec_done, vec.at("A cum"))
                dve.tensor_tensor(g[:, GU], g[:, GI], g[:, CUM], ALU.subtract).then_inc(vec_done, vec("A u"))
                dve.wait_ge(vec_done, vec.at("A u"))
                dve.tensor_tensor_scan(g[:, GM], one, g[:, GU], 0.0, ALU.mult, ALU.max).then_inc(vec_done, vec("A max"))
                dve.wait_ge(vec_done, vec.at("A max"))
                dve.tensor_tensor(g[:, GE], g[:, CUM], g[:, GM], ALU.add).then_inc(vec_done, vec("A em"))
                dve.tensor_scalar(g[:, GM], g[:, GM], -1.0, None, ALU.mult).then_inc(vec_done, vec("A -m"))
                evac(a_k[:, 0:2], u + 3)
                split(u + 6)
                evac(a_k[:, 2:4], u + 4)
                split(u + 7)
                dve.wait_ge(pe_done, pe_.at("A u_col"))
                dve.tensor_copy(u_col, ps[:, STAT, 0:8]).then_inc(vec_done, vec("A u_col"))
                evac(a_vt[:, 0:2], u + 5)
                split(u + 8)
                for h in range(4):
                    dve.wait_ge(pe_done, pe_.at(f"A s {h}"))
                    dve.wait_ge(pool_done, pool_.at(f"A e {h} 1"))
                    dve.tensor_tensor(a_s[:, h], ps[:, h, 0:384], a_e[:, h], ALU.mult).then_inc(vec_done, vec(f"A s {h}"))
                evac(a_vt[:, 2:4], u + 6)
                split(u + 9)
                evac(a_vt[:, 4:6], u + 7)
                split(u + 10)
                dve.wait_ge(pe_done, pe_.at("A den"))
                dve.wait_ge(act_done, act_.at("A em"))
                dve.scalar_tensor_tensor(out=g[:, GL], in0=ps[0:4, STAT, 0:T], scalar=-1.0, in1=g[:, GE], op0=ALU.mult,
                                         op1=ALU.max).then_inc(vec_done, vec("A -den"))
                dve.wait_ge(vec_done, vec.at("A -den"))
                dve.tensor_tensor(g[:, GL], ps[0:4, STAT, 0:T], g[:, GL], ALU.max).then_inc(vec_done, vec("A den"))
                dve.wait_ge(vec_done, vec.at("A den"))
                dve.reciprocal(g[:, GL], g[:, GL]).then_inc(vec_done, vec("A rden"))
                evac(a_vt[:, 6:8], u + 8)
                split(u + 11)
                evac(xq_a[:, 0:2], u + 9)
                split(u + 12)
                evac(xq_a[:, 2:4], u + 10)
                split(u + 13)
                for h in range(4):
                    dve.wait_ge(pe_done, pe_.at(f"A num {h}"))
                    dve.wait_ge(act_done, act_.at("A rden 1"))
                    dve.tensor_tensor(a_h[:, 2 * h:2 * h + 2], tiles(ps[:, h, :]), wide(a_rden[:, h]),
                                      ALU.mult).then_inc(vec_done, vec(f"A h {h}"))
                evac(a_o[:, 0:2], u + 11)
                split(u + 14)
                query_root("A")
                dve.wait_ge(pe_done, pe_.at("A hsum"))
                root(KB(28, 4), ps[:, 0:2, :].rearrange("p a b -> p (a b)"), KB(24, 4), KB(28, 4), KB(32, 4), 1.0 / T, name="A heads")
                evac(a_o[:, 2:4], u + 12)
                split(u + 15)
                mem_max("A")
                for k in range(8):
                    dve.scalar_tensor_tensor(out=a_h[:, k], in0=a_h[:, k], scalar=col("h_norm", k), in1=tiles(KB(28, 4))[:, k // 2],
                                             op0=ALU.mult, op1=ALU.mult).then_inc(vec_done, vec(f"A hn {k}"))

                def gated(j):
                    dve.wait_ge(pool_done, pool_.at(f"A gate {j}"))
                    dve.wait_ge(vec_done, vec.at(f"A hn {2 * j + 1}"))
                    dve.tensor_tensor(a_h[:, 2 * j:2 * j + 2], a_h[:, 2 * j:2 * j + 2], a_o[:, 2 * j:2 * j + 2],
                                      ALU.mult).then_inc(vec_done, vec(f"A y {j}"))

                gated(0)
                gated(1)
                mem_probs("A", p_a)
                low_a(0)
                low_a(1)
                evac(a_o[:, 4:6], u + 13)
                split(u + 16)
                gated(2)
                low_a(2)
                evac(a_o[:, 6:8], u + 14)
                split(v + 2)
                gated(3)
                low_a(3)
                split(v + 3)
                mem_low("A", 4)
                for j in range(4, 8):
                    split(v + j)

            def mixb(n, gain, factor):
                u, v = U["mixb"], U["mixb_out"]
                norm(n, gain, factor, u - 1)
                split(u + 2)
                split(u + 3)
                token_root(n)

                def sine(j):
                    t0, w = B_STEPS[j]
                    dve.wait_ge(pe_done, pe_.at(f"B rot {j}"))
                    if j > 1:
                        dve.wait_ge(pool_done, pool_.at(f"B x {j - 2}"))
                    dve.tensor_tensor(tiles(b_rot[:, j % 2])[:, 0:w], tiles(rot_bank(j)[:, 0:w * T]), wide(rope[:, 1, :], w),
                                      ALU.mult).then_inc(vec_done, vec(f"B sin {j}"))

                def window_scores(b):
                    for h in range(4 * b, 4 * b + 4):
                        dve.wait_ge(pe_done, pe_.at(f"B s {h}"))
                        if h >= 8:
                            dve.wait_ge(pe_done, pe_.at(f"B pT {h - 8}"))
                        dve.tensor_tensor(b_s[:, h % 8], ps[:, BANK["S", h], 0:384], window[:, :], ALU.add).then_inc(vec_done, vec(f"B s {h}"))

                def maxima(b):
                    for h in range(4 * b, 4 * b + 4):
                        for blk, (lo, hi) in enumerate(BLOCKS):
                            dve.wait_ge(vec_done, vec.at(f"B s {h}"))
                            dve.tensor_reduce(b_stat[:, 0, h, blk:blk + 1], b_s[:, h % 8, lo:hi], AXX, ALU.max).then_inc(vec_done, vec(f"B max {h} {blk}"))
                    m, neg, _, sk, _ = (b_stat[:, k, 4 * b:4 * b + 4] for k in range(5))
                    r = b_r[:, :, 4 * b:4 * b + 4].rearrange("p b h -> p h b")
                    sink = sinks[:, 4 * b:4 * b + 4].unsqueeze(2).broadcast_to([P, 4, 2])
                    dve.wait_ge(vec_done, vec.at(f"B max {4 * b + 3} 1"))
                    dve.tensor_tensor(m, m, r, ALU.mult).then_inc(vec_done, vec(f"B mr {b}"))
                    dve.wait_ge(vec_done, vec.at(f"B mr {b}"))
                    dve.tensor_tensor(m, m, sink, ALU.max).then_inc(vec_done, vec(f"B m {b}"))
                    dve.wait_ge(vec_done, vec.at(f"B m {b}"))
                    dve.tensor_scalar(neg, m, -1.0, None, ALU.mult).then_inc(vec_done, vec(f"B -m {b}"))
                    dve.tensor_tensor(sk, sink, m, ALU.subtract).then_inc(vec_done, vec(f"B sink {b}"))

                def probs(b):
                    _, _, den, sk, inv = (b_stat[:, k, 4 * b:4 * b + 4] for k in range(5))
                    dve.wait_ge(act_done, act_.at(f"B sink {b}"))
                    dve.tensor_tensor(den, den, sk, ALU.add).then_inc(vec_done, vec(f"B den {b}"))
                    dve.wait_ge(vec_done, vec.at(f"B den {b}"))
                    dve.reciprocal(inv, den).then_inc(vec_done, vec(f"B inv {b}"))
                    dve.wait_ge(vec_done, vec.at(f"B inv {b}"))
                    for h in range(4 * b, 4 * b + 4):
                        for blk, (lo, hi) in enumerate(BLOCKS):
                            s = b_s[:, h % 8, lo:hi]
                            dve.tensor_scalar(s, s, b_stat[:, 4, h, blk:blk + 1], None, ALU.mult).then_inc(vec_done, vec(f"B p {h} {blk}"))

                def low(b):
                    dve.wait_ge(act_done, act_.at(f"B hi {b}"))
                    dve.tensor_tensor(y_lo[:, 2 * b:2 * b + 2], tiles(ps[:, STAT, :]), y_hi[:, 2 * b:2 * b + 2].bitcast(F32),
                                      ALU.subtract).then_inc(vec_done, vec(f"B lo {b}"))

                evac(xq_b[:, 0:2], u)
                evac(xq_b[:, 2:4], u + 1)
                split(u + 4)
                evac(b_x[:, 8:10], u + 2)
                split(u + 5)
                query_root("B")
                evac(b_x[:, 0:2], u + 3)
                mem_max("B")
                dve.wait_ge(pe_done, pe_.at("B sum"))
                root(b_ry, ps[:, STAT, T:], b_rv, b_ry, b_rt, 1.0 / B_HD)
                dve.scalar_tensor_tensor(out=b_x[:, 8], in0=b_x[:, 8], scalar=col("b_k"), in1=b_ry, op0=ALU.mult,
                                         op1=ALU.mult).then_inc(vec_done, vec("B n 0"))
                split(u + 6)
                mem_probs("B", p_b)
                evac(b_x[:, 2:4], u + 4)
                sine(0)
                split(v)
                evac(b_x[:, 4:6], u + 5)
                sine(1)
                split(v + 1)
                mem_low("B", 0)
                evac(b_x[:, 6:8], u + 6)
                sine(2)
                sine(3)
                window_scores(0)
                sine(4)
                dve.wait_ge(pe_done, pe_.at("B qsum"))
                dve.tensor_copy(b_rows, ps[0:16, STAT, 0:T]).then_inc(vec_done, vec("B qsum"))
                dve.wait_ge(pe_done, pe_.at("B qcol"))
                q_v, q_t = b_rvt[:, 0:32], b_rvt[:, 32:64]
                root(b_r[:, :, :].rearrange("p a b -> p (a b)"), ps[:, STAT, T:T + 32], q_v, b_r[:, :, :].rearrange("p a b -> p (a b)"), q_t, 1.0 / B_HD)
                maxima(0)
                split(v + 2)
                window_scores(1)
                probs(0)
                maxima(1)
                probs(1)
                split(v + 3)
                low(0)
                split(v + 4)
                low(1)
                window_scores(2)
                window_scores(3)
                maxima(2)
                probs(2)
                split(v + 5)
                maxima(3)
                low(2)
                probs(3)
                split(v + 6)
                low(3)
                split(v + 7)

            def ssd(n, gain, factor):
                u = U["dt"]
                norm(n, gain, factor, u - 1)
                split(u + 2)
                split(u + 3)
                token_root(n)
                dve.wait_ge(w_used, u + 1)
                dve.tensor_tensor(s_dtx, ps[0:32, bank(u), 0:T], rstd[0:32, :], ALU.mult).then_inc(drained[u % RING], 1)
                dve.wait_ge(drained[u % RING], fills[u])
                dve.tensor_scalar(s_dtx, s_dtx, dt_bias, None, ALU.add).then_inc(vec_done, vec("S dt x"))
                dve.wait_ge(vec_done, vec.at("S dt x"))
                dve.scalar_tensor_tensor(out=s_dtl, in0=s_dtx, scalar=-1.0, in1=s_dtx, op0=ALU.mult, op1=ALU.min).then_inc(vec_done, vec("S -abs"))
                for e in range(2):
                    dve.tensor_scalar(d_half[64 * e:64 * e + 64], d_all[64 * e:64 * e + 64].rearrange("p (j e) -> p e j", e=2)[:, e], 0.5, None,
                                      ALU.mult).then_inc(vec_done, vec(f"S d {e}"))

                def dt_rows():
                    dve.wait_ge(act_done, act_.at("S softplus"))
                    dve.scalar_tensor_tensor(out=s_dt, in0=s_dtx, scalar=0.0, in1=s_dtl, op0=ALU.max, op1=ALU.add).then_inc(vec_done, vec("S dt"))
                    dve.wait_ge(vec_done, vec.at("S dt"))
                    dve.tensor_scalar(s_dA, s_dt, a_log, -1.0, ALU.mult, ALU.mult).then_inc(vec_done, vec("S dA"))
                    dve.tensor_scalar(s_dth, s_dt, 0.5, None, ALU.mult).then_inc(vec_done, vec("S dt half"))
                    dve.wait_ge(vec_done, vec.at("S dA"))
                    for b in range(2):
                        blk = slice(b * P, b * P + P)
                        dve.tensor_tensor_scan(s_A[:, blk], ones[0:32, 0:1].broadcast_to([32, P]), s_dA[:, blk], 0.0, ALU.mult,
                                               ALU.add).then_inc(vec_done, vec(f"S A {b}"))
                    dve.wait_ge(vec_done, vec.at("S A 1"))
                    dve.tensor_copy(select[:, :], ident[0:32, 0:32]).then_inc(vec_done, vec("S select"))
                    dve.tensor_copy(A_hi, s_A).then_inc(vec_done, vec("S A hi"))
                    dve.wait_ge(vec_done, vec.at("S A hi"))
                    dve.tensor_tensor(A_lo, s_A, A_hi.bitcast(F32), ALU.subtract).then_inc(vec_done, vec("S A lo"))
                    dve.tensor_scalar(s_nA, s_A, -1.0, None, ALU.mult).then_inc(vec_done, vec("S -A"))
                    dve.wait_ge(vec_done, vec.at("S -A"))
                    dve.tensor_scalar(s_cross[:, 0:P], s_nA[:, 0:P], s_A[:, P - 1:P], None, ALU.add).then_inc(vec_done, vec("S cross"))

                def evac_conv(c):
                    q = 2 * (c % 2)
                    if c > 1:
                        dve.wait_ge(pool_done, pool_.at(f"S x {c - 2}"))
                    evac(s_in[:, q:q + 2], U["bc"] + c)

                def taps(c):
                    q, k0 = 2 * (c % 2), U["bc"] + c
                    for tap_ in (2, 1, 0):
                        s = 3 - tap_
                        for t in range(2):
                            if tap_ == 2:
                                dve.wait_ge(act_done, act_.at(f"S tap {c} {t}"))
                                dve.wait_ge(drained[k0 % RING], fills[k0])
                            else:
                                dve.wait_ge(vec_done, vec.at(f"S tap{tap_ + 1} {c} {t}"))
                            dve.scalar_tensor_tensor(out=s_cv[:, q + t, s:], in0=s_in[:, q + t, 0:T - s], scalar=col(f"conv_w{tap_}", conv_tile(c) + t),
                                                     in1=s_cv[:, q + t, s:], op0=ALU.mult, op1=ALU.add).then_inc(vec_done, vec(f"S tap{tap_} {c} {t}"))

                def times_dt(j):
                    dve.wait_ge(pe_done, pe_.at(f"S xT {j}"))
                    for tt in range(2):
                        dst = s_xdt[:, tt, 256 * j:256 * j + 256].rearrange("p (h e) -> p h e", e=64)
                        dtc = dt_col[:, 32 * tt + 4 * j:32 * tt + 4 * j + 4].unsqueeze(2).broadcast_to([P, 4, 64])
                        dve.tensor_tensor(dst, ps[:, STAT, tt * T:tt * T + T].rearrange("p (h e) -> p h e", e=64), dtc,
                                          ALU.mult).then_inc(vec_done, vec(f"S xdt {j} {tt}"))

                def segments(j):
                    for h in range(4 * j, 4 * j + 4):
                        dve.wait_ge(pe_done, pe_.at(f"S A {h | 1}"))
                        if h > 5:
                            dve.wait_ge(pe_done, pe_.at(f"S y {h - 6}"))
                        for b in (0, 1):
                            dve.wait_ge(vec_done, vec.at("S bias_col"))
                            dve.tensor_scalar(s_e[:, h % 6, 2 * b * P:2 * b * P + P], half(h % 4 // 2, h)[:, b * P:b * P + P],
                                              bias_col[:, 32 * b + h:32 * b + h + 1], 0.0, ALU.add, ALU.min).then_inc(vec_done, vec(f"S seg {h} {2 * b}"))

                def skip(j):
                    for t in range(2):
                        k = 2 * j + t
                        dve.wait_ge(pe_done, pe_.at(f"S y {4 * j + 3}"))
                        dve.scalar_tensor_tensor(out=s_x[:, k], in0=s_x[:, k], scalar=d_half[:, k:k + 1], in1=ps[:, 2 + j % 2, t * T:t * T + T],
                                                 op0=ALU.mult, op1=ALU.add).then_inc(vec_done, vec(f"S y {k}"))

                def gate_z(i):
                    z = s_z[:, 2 * (i % 2):2 * (i % 2) + 2]
                    dve.wait_ge(act_done, act_.at(f"S zth {i}"))
                    dve.scalar_tensor_tensor(out=z, in0=s_zth[:, 2 * (i % 2):2 * (i % 2) + 2], scalar=1.0, in1=z, op0=ALU.add,
                                             op1=ALU.mult).then_inc(vec_done, vec(f"S z {i}"))
                    dve.wait_ge(vec_done, vec.at(f"S z {i}"))
                    dve.wait_ge(vec_done, vec.at(f"S y {2 * i + 1}"))
                    dve.tensor_tensor(s_x[:, 2 * i:2 * i + 2], s_x[:, 2 * i:2 * i + 2], z, ALU.mult).then_inc(vec_done, vec(f"S yz {i}"))

                def group_root(i):
                    dve.wait_ge(pe_done, pe_.at(f"S zsum {4 * i + 3}"))
                    root(g_y, ps[:, STAT if i == 0 else 1, :], g_v, g_y, g_t, 1.0 / 512, 4 * EPS)

                def normed(ks):
                    for k in ks:
                        dve.scalar_tensor_tensor(out=s_x[:, k], in0=s_x[:, k], scalar=col("ssd_norm", k), in1=tiles(g_y)[:, k // 4 % 2],
                                                 op0=ALU.mult, op1=ALU.mult).then_inc(vec_done, vec(f"S yn {k}"))

                def lows(ks):
                    for k in ks:
                        dve.wait_ge(act_done, act_.at(f"S hi {k}"))
                        dve.tensor_tensor(y_lo[:, k], s_x[:, k], y_hi[:, k].bitcast(F32), ALU.subtract).then_inc(vec_done, vec(f"S lo {k}"))

                for c in range(28):
                    if c:
                        split(U["bc"] + c + 2)
                    if c == 1:
                        dt_rows()
                    if c == 4:
                        dve.wait_ge(pe_done, pe_.at("S cols"))
                        dve.tensor_copy(dt_col, ps[:, STAT, 0:64]).then_inc(vec_done, vec("S dt_col"))
                        dve.tensor_copy(bias_col, ps[:, STAT, 64:160]).then_inc(vec_done, vec("S bias_col"))
                    if c in (7, 8):
                        for g in (2 * c - 14, 2 * c - 13):
                            dve.wait_ge(pe_done, pe_.at(f"S CB {g}"))
                            dve.scalar_tensor_tensor(out=s_cb[:, g], in0=ps[:, g, 0:384], scalar=0.25, in1=mask[:, :], op0=ALU.mult,
                                                     op1=ALU.mult).then_inc(vec_done, vec(f"S CB {g}"))
                    if 1 <= c <= 12:
                        taps(c - 1)
                    if 9 <= c < 17:
                        segments(c - 9)
                    if 9 <= c < 17:
                        times_dt(c - 9)
                    if 11 <= c < 19:
                        skip(c - 11)
                    if 13 <= c < 21:
                        gate_z(c - 13)
                    if c in (19, 23):
                        group_root((c - 19) // 4)
                    if c == 21:
                        normed(range(0, 8))
                    if c == 22:
                        lows(range(0, 4))
                    if c == 24:
                        normed(range(8, 12))
                        lows(range(4, 6))
                    if c == 25:
                        normed(range(12, 16))
                        lows(range(6, 8))
                    if c > 25:
                        lows(range(4 * c - 96, 4 * c - 92))
                    if c < 12:
                        evac_conv(c)
                    elif c < 20:
                        dve.wait_ge(pool_done, pool_.at(f"S zsq {c - 14}" if c > 13 else f"S x {c - 2}"))
                        evac(s_z[:, 2 * (c % 2):2 * (c % 2) + 2], U["z"] + c - 12)
                    elif c < 24:
                        evac(tiles(s_gate[:, c - 20]), U["ga"] + c - 20)
                    else:
                        dve.wait_ge(pool_done, pool_.at("S zsq 7"))
                        evac(s_gate_b[c - 24], U["gb"] + c - 24)
                for j in range(4):
                    k = U["aproj"] + 2 * j
                    split(k + 2)
                    split(k + 3)
                    dve.wait_ge(w_used, k + 2)
                    dve.wait_ge(act_done, act_.at(f"S ga {j}"))
                    dve.scalar_tensor_tensor(out=s_merged[:, 2 * j:2 * j + 2], in0=tiles(s_gate[:, j]), scalar=1.0, in1=tiles(ps[:, bank(k), :]),
                                             op0=ALU.add, op1=ALU.mult).then_inc(drained[k % RING], 1)
                u = U["sconv"]
                r2 = rs_v[:, :]
                dve.tensor_tensor(r2, rstd[:, :], rstd[:, :], ALU.mult).then_inc(vec_done, vec("S r2"))
                dve.wait_ge(vec_done, vec.at("S r2"))

                def conv_gated(j):
                    k, q = u + 3 * j, j % 2
                    dve.wait_ge(drained[(k + 2) % RING], fills[k + 2])
                    dve.wait_ge(vec_done, vec.at(f"S stap0 {j} 1"))
                    dve.tensor_tensor(sc_b[:, q], sc_b[:, q], sc_v[:, q], ALU.mult).then_inc(vec_done, vec(f"S sy {j}"))

                for j in range(4):
                    k, q = u + 3 * j, j % 2
                    split(k + 2)
                    if j:
                        conv_gated(j - 1)
                    evac(tiles(sc_c[:, q]), k, r=r2)
                    split(k + 3)
                    if j:
                        s_low(j - 1)
                    dve.wait_ge(w_used, k + 2)
                    dve.wait_ge(drained[k % RING], fills[k])
                    dve.tensor_tensor(sc_prod[:, q], ps[:, bank(k + 1), :], sc_c[:, q], ALU.mult).then_inc(drained[(k + 1) % RING], 1)
                    split(k + 4)
                    for tap in (1, 0):
                        s = 2 - tap
                        for t in range(2):
                            v, p = tiles(sc_v[:, q])[:, t], tiles(sc_prod[:, q])[:, t]
                            if tap == 1:
                                dve.wait_ge(act_done, act_.at(f"S stap {j} {t}"))
                                dve.wait_ge(drained[(k + 1) % RING], fills[k + 1])
                            else:
                                dve.wait_ge(vec_done, vec.at(f"S stap1 {j} {t}"))
                            dve.scalar_tensor_tensor(out=v[:, s:], in0=p[:, 0:T - s], scalar=col(f"sconv_w{tap}", 2 * j + t), in1=v[:, s:],
                                                     op0=ALU.mult, op1=ALU.add).then_inc(vec_done, vec(f"S stap{tap} {j} {t}"))
                    evac(tiles(sc_b[:, q]), k + 2)
                conv_gated(3)
                for j in range(4):
                    k, m = U["sproj"] + j, slice(2 * j, 2 * j + 2)
                    if j == 0:
                        s_low(3)
                    split(k + 2)
                    dve.wait_ge(w_used, k + 1)
                    dve.wait_ge(act_done, act_.at(f"S gb {j}"))
                    dve.scalar_tensor_tensor(out=tiles(s_br[:, j % 2]), in0=s_gate_b[j], scalar=1.0, in1=tiles(ps[:, bank(k), :]),
                                             op0=ALU.add, op1=ALU.mult).then_inc(drained[k % RING], 1)
                    dve.wait_ge(drained[k % RING], fills[k])
                    dve.tensor_tensor(s_merged[:, m], s_merged[:, m], tiles(s_br[:, j % 2]), ALU.add).then_inc(vec_done, vec(f"S merged {j}"))
                    dve.wait_ge(act_done, act_.at(f"S mhi {j}"))
                    dve.tensor_tensor(xg_lo[:, m], s_merged[:, m], xg_hi[:, m].bitcast(F32), ALU.subtract).then_inc(vec_done, vec(f"S mlo {j}"))
                for j in range(4):
                    split(U["w_o"] + j + 2)

            def s_low(j):
                dve.wait_ge(act_done, act_.at(f"S shi {j}"))
                dve.tensor_tensor(y_lo[:, 2 * j:2 * j + 2], tiles(sc_b[:, j % 2]), y_hi[:, 2 * j:2 * j + 2].bitcast(F32),
                                  ALU.subtract).then_inc(vec_done, vec(f"S slo {j}"))

            def low_a(j):
                dve.wait_ge(act_done, act_.at(f"A hi {j}"))
                dve.tensor_tensor(y_lo[:, 2 * j:2 * j + 2], a_h[:, 2 * j:2 * j + 2], y_hi[:, 2 * j:2 * j + 2].bitcast(F32),
                                  ALU.subtract).then_inc(vec_done, vec(f"A lo {j}"))

            dve.memset(block_ones[:, :], 0.0).then_inc(vec_done, vec("block_ones 0"))
            dve.memset(head_rows[:, :, :], 0.0).then_inc(vec_done, vec("head_rows 0"))
            dve.wait_ge(vec_done, vec.at("head_rows 0"))
            for j in range(2):
                dve.memset(block_ones[64 * j:64 * j + 64, 64 * j:64 * j + 64], 1.0).then_inc(vec_done, vec(f"block_ones {j + 1}"))
            for h in range(4):
                dve.memset(head_rows[:, h, h:h + 1], 1.0).then_inc(vec_done, vec(f"head_rows {h + 1}"))
            dve.memset(pair_rows[:, :], 0.0).then_inc(vec_done, vec("pair_rows 0"))
            dve.wait_ge(vec_done, vec.at("pair_rows 0"))
            for j in range(2):
                dve.memset(pair_rows[64 * j:64 * j + 64, 16 + j:17 + j], 1.0).then_inc(vec_done, vec(f"pair_rows {j + 1}"))
            dve.wait_ge(pe_done, pe_.at("mem gain"))
            dve.tensor_copy(cols[:, 0, 0:8], ps[:, STAT, 0:8]).then_inc(vec_done, vec("mem gain"))
            for name, gain, factor in PHASES:
                n = norm_of[name][0]
                if name.startswith("ffn"):
                    ffn(int(name[3:]), n, gain, factor)
                elif name != "final":
                    {"mem": mem, "mixa": mixa, "mixb": mixb, "ssd": ssd}[name](n, gain, factor)
            n, gain, factor = norm_of["final"]
            norm(n, gain, factor, NU - 1, split_x=False)
            for k in range(DT):
                dve.wait_ge(x_new, 4 * n + 4)
                dve.tensor_scalar(x_gain[:, k], x[:, k], col(gain, k), None, ALU.mult).then_inc(vec_done, vec(f"x gain {k}"))
            dve.wait_ge(stat_done, n + 1)
            root(fin_r, ps[:, STAT, 0:2], fin_v, fin_r, fin_t, 1.0 / D)
            dve.wait_ge(pe_done, pe_.at("out"))
            for c in (0, 2):
                dve.tensor_scalar(yout[:, c // 2, 0:512], ps[:, c, :], fin_r[:, c // 2:c // 2 + 1], None,
                                  ALU.mult).then_inc(vec_done, vec(f"out {c}"))

        @block.tensor
        def _(pe):
            def block_passes(dst, wsl, w_at, xh, xl, start, stop, inc=None):
                s = wsl
                hi, lo = w_hi[:, s, w_at:w_at + P], w_lo[:, s, w_at:w_at + P]
                pe.matmul(dst, hi, xh, start=start, stop=False, skip_group_check=True)
                pe.matmul(dst, hi, xl, start=False, stop=False, skip_group_check=True)
                last = pe.matmul(dst, lo, xh, start=False, stop=stop, skip_group_check=True)
                return last

            def g_unit(u, i=0, X=None, kt0=0, offs=(0, P), into=None, norm=None, opens=True, ready=None):
                s, b = u % RING, 4 + (u if into is None else into) % RING
                xh, xl = X or (xg_hi, xg_lo)
                pe.wait_ge(w_split, u + 1 + 6 * i)
                if opens and fills[u] > 1:
                    pe.wait_ge(drained[s], fills[u] - 1 + 2 * i)
                for n, off in enumerate(offs):
                    for k in range(8):
                        if norm is not None and n == 0:
                            pe.wait_ge(xl_ready, 8 * norm + k + 1)
                        if ready and n == 0:
                            ready(k)
                        last = block_passes(ps[:, b, n * T:n * T + T], s, k * 256 + off, xh[:, kt0 + k],
                                            xl[:, kt0 + k], opens and n == 0 and k == 0, k == 7)
                last.then_inc(w_used, 1)

            def d_unit(u, i=0, Y=None, y0=0, start=False, norm=None):
                s = u % RING
                yh, yl = Y or (y_hi, y_lo)
                pe.wait_ge(w_split, u + 1 + 6 * i)
                for m in range(8):
                    for k in range(2):
                        last = block_passes(ps[:, m // 2, (m % 2) * T:(m % 2) * T + T], s, k * D + m * P,
                                            yh[:, y0 + k], yl[:, y0 + k], start and m % 2 == 0 and k == 0,
                                            k == 1)
                    if norm is not None and m in (1, 3, 5):
                        last.then_inc(acc_ready, 1)
                last.then_inc(w_used, 1)

            def stat(n):
                pe.wait_ge(sq_summed, 3 * n + 3)
                pe.matmul(ps[:, STAT, 0:T], ones[:, :], sq[:, 0, 0:T], start=True, stop=False)
                pe.matmul(ps[:, STAT, 0:T], ones[:, :], sq[:, 0, T:2 * T], start=False, stop=True).then_inc(stat_done, 1)

            def turn(src, n):
                for k in range(DT):
                    for tt in range(2):
                        o = (k % 2) * T + tt * P
                        last = pe.transpose(ps[:, k // 2, o:o + P], src[:, tt, k * P:k * P + P], ident[:, :])
                    if k % 2:
                        last.then_inc(turned if k == DT - 1 else acc_ready, 1)

            def ffn(f, n):
                u = U[f"ffn{f}"]
                g_unit(u, norm=n)
                if f == 0:
                    mem_values(u - 2)
                g_unit(u + 1)
                stat(n)

                def down(v, i, p, it=0, **kw):
                    pe.wait_ge(ffn_hl, NI * nth[f] + i + 1)
                    d_unit(v, it, y0=2 * p, **kw)

                for i in (1, 2):
                    g_unit(u + 3 * i - 1)
                    g_unit(u + 3 * i)
                    if f == 0 and i == 1:
                        pe.wait_ge(act_done, act_.at("M v 1"))
                        pe.wait_ge(vec_done, vec.at("M ksum"))
                    down(u + 3 * i + 1, i - 1, (i - 1) % 2, start=i == 1)
                with pe.Fori(0, (NI - 3) // 2) as b:
                    for j in range(2):
                        g_unit(u + 8 + 3 * j, b)
                        g_unit(u + 9 + 3 * j, b)
                        down(u + 10 + 3 * j, 2 * b + 2 + j, j, b)
                down(u + 3 * NI - 1, NI - 1, 0, norm=n + 1)

            def mem(n):
                u = U["mem"]
                g_unit(u, norm=n)
                pe.wait_ge(loaded, 16 * N_SMALL)
                for tile in range(3):
                    last = pe.transpose(ps[:, 3, tile * P:tile * P + P], rows[:, tile, :], ident[:, :])
                last.then_inc(pe_done, pe_("vectors"))
                g_unit(u + 1)
                stat(n)
                pe.wait_ge(x_loaded, 16)
                pe.wait_ge(vec_done, vec.at("cols"))
                turn(xin, n + 1)
                g_unit(u + 2)
                pe.wait_ge(x_new, 8)
                for h in range(4):
                    pe.wait_ge(act_done, act_.at(f"M sq {h // 2}"))
                    last = pe.matmul(ps[:, h // 2, (h % 2) * T:(h % 2) * T + T], ones[:, :], tiles(KB(40, 4))[:, h],
                                     start=True, stop=True)
                last.then_inc(pe_done, pe_("M ksum"))
                g_unit(u + 3)

            def mem_values(u):
                for mt in range(2):
                    for k in range(4):
                        evacuated(u + k // 2)
                        last = pe.transpose(ps[:, 2 + mt, k * P:k * P + P], tiles(KB(32, 4))[:, k, mt * P:mt * P + P], ident[:, :])
                last.then_inc(pe_done, pe_("M v"))

            def evacuated(u):
                pe.wait_ge(drained[u % RING], fills[u])

            def selector(h, rows_=4):
                return ident[0:rows_, h:h + 1].broadcast_to([rows_, P])

            def query_sums(tag, xsq):
                for h in range(4):
                    pe.wait_ge(act_done, act_.at(f"{tag} xsq {h // 2}"))
                    for tt in range(2):
                        last = pe.matmul(ps[:, STAT, 2 * h + tt:2 * h + tt + 1], xsq[:, h, tt * P:tt * P + P], ones[:, 0:1], start=True, stop=True)
                last.then_inc(pe_done, pe_(f"{tag} xsum"))

            def mem_scores(tag, xq):
                for h in range(4):
                    pe.wait_ge(act_done, act_.at(f"{tag} xq {h // 2}"))
                    for tt in range(2):
                        last = pe.matmul(half(h, tt), xq[:, h, tt * P:tt * P + P], mem_k[:, h], start=True, stop=True)
                    last.then_inc(pe_done, pe_(f"{tag} m s {h}"))

            def mem_turn(tag, p, base, free):
                free()
                for h in range(4):
                    for tt in range(2):
                        pe.wait_ge(vec_done, vec.at(f"{tag} m p {2 * h + tt}"))
                        for mt in range(2):
                            last = pe.transpose(half(base + h, mt)[:, tt * P:tt * P + P], p[:, 2 * h + tt, mt * P:mt * P + P], ident[:, :])
                    last.then_inc(pe_done, pe_(f"{tag} m pT {h}"))

            def mem_out(tag, pt, base):
                pe.wait_ge(act_done, act_.at(f"{tag} m pT 3"))
                for h in range(4):
                    for mt in range(2):
                        last = pe.matmul(half(base + h // 2, h), mem_v[:, mt, h * P:h * P + P], pt[:, 2 * h + mt],
                                         start=mt == 0, stop=mt == 1)
                last.then_inc(pe_done, pe_(f"{tag} m o"))

            def mixa(n):
                u, v = U["mixa"], U["mixa_out"]
                g_unit(u, offs=(0, 4), norm=n)
                g_unit(u + 1)
                stat(n)
                g_unit(u + 2)
                g_unit(u + 3)
                g_unit(u + 4)
                pe.wait_ge(vec_done, vec.at("A -m"))
                g = a_rows[0:4]
                for tt in range(2):
                    last = pe.transpose(ps[:, STAT, 4 * tt:4 * tt + 4], g[:, GU, tt * P:tt * P + P], ident[0:4, 0:4])
                last.then_inc(pe_done, pe_("A u_col"))
                for h in range(4):
                    last = pe.matmul(half(h // 2, h), selector(h), g[:, GM], start=True, stop=True)
                last.then_inc(pe_done, pe_("A -m"))
                g_unit(u + 5)
                evacuated(u + 4)
                for h in range(4):
                    pe.wait_ge(act_done, act_.at("A e 3"))
                    pe.matmul(ps[:, h, 0:T], a_k[:, h, 0:P], a_q[:, h], start=True, stop=True)
                    pe.matmul(ps[:, h, T:384], a_k[:, h, P:], a_q[:, h, P:], start=True,
                              stop=True).then_inc(pe_done, pe_(f"A s {h}"))
                g_unit(u + 6)
                g_unit(u + 7)
                for h in range(4):
                    pe.wait_ge(vec_done, vec.at(f"A s {h}"))
                    pe.matmul(ps[0:4, STAT, 0:T], head_rows[:, h, :], a_s[:, h, 0:T], start=h == 0, stop=False, skip_group_check=True)
                    last = pe.matmul(ps[0:4, STAT, P:T], head_rows[:, h, :], a_s[:, h, T:], start=False, stop=h == 3, skip_group_check=True)
                last.then_inc(pe_done, pe_("A den"))
                g_unit(u + 8)
                pe.wait_ge(vec_done, vec.at("A rden"))
                for j in range(2):
                    if j:
                        pe.wait_ge(act_done, act_.at("A rden 0"))
                    for h in (2 * j, 2 * j + 1):
                        last = pe.matmul(half(STAT, h), selector(h), g[:, GL], start=True, stop=True)
                    last.then_inc(pe_done, pe_(f"A rden {j}"))
                    g_unit(u + 9 + j)
                    if j == 0:
                        evacuated(u + 8)
                        for b in range(4):
                            for k in range(4):
                                last = pe.transpose(ps[:, b, k * P:k * P + P], a_vt[:, 4 * (b % 2) + k, (b // 2) * P:(b // 2) * P + P], ident[:, :])
                        last.then_inc(pe_done, pe_("A v"))
                for h in range(4):
                    pe.wait_ge(act_done, act_.at("A v 3"))
                    for e in range(2):
                        c = h * T + e * P
                        pe.matmul(half(h, e), a_v[:, 0, c:c + P], a_s[:, h, 0:T], start=e == 0, stop=False, skip_group_check=True)
                        last = pe.matmul(half(h, e)[:, P:], a_v[:, 1, c:c + P], a_s[:, h, T:], start=False, stop=e == 1, skip_group_check=True)
                    last.then_inc(pe_done, pe_(f"A num {h}"))
                g_unit(u + 11)
                pe.wait_ge(vec_done, vec.at("A h 3"))
                query_sums("A", xsq_a)
                for h in range(4):
                    pe.wait_ge(act_done, act_.at(f"A hsq {h}"))
                    for e in range(2):
                        last = pe.matmul(half(h // 2, h), ones[:, :], a_hsq[:, 2 * h + e], start=e == 0, stop=e == 1)
                last.then_inc(pe_done, pe_("A hsum"))
                g_unit(u + 12)
                pe.wait_ge(rs_vec, root_.at("A heads"))
                mem_scores("A", xq_a)
                g_unit(u + 13)
                g_unit(u + 14)

                def out_unit(j, **kw):
                    pe.wait_ge(vec_done, vec.at(f"A lo {j}" if j < 4 else "A m lo"))
                    if j == 0:
                        pe.wait_ge(act_done, act_.at("A m exp 7"))
                    d_unit(v + j, y0=2 * j, start=j == 0, norm=n + 1 if j == 5 else None)

                out_unit(0)

                def free():
                    for j in (12, 13, 14):
                        evacuated(u + j)
                mem_turn("A", p_a, 4, free)
                out_unit(1)
                mem_out("A", pt_a, 4)
                for j in range(2, 6):
                    out_unit(j)

            def mixb(n):
                u, v = U["mixb"], U["mixb_out"]

                def pair(j):
                    t0, w = B_STEPS[j]
                    if j:
                        pe.wait_ge(act_done, act_.at(f"B n {j}"))
                    else:
                        pe.wait_ge(vec_done, vec.at("B n 0"))
                    if j > 2:
                        pe.wait_ge(vec_done, vec.at(f"B sin {j - 2}"))
                    pe.matmul(rot_bank(j)[:, 0:w * T], rotate[:, :], b_x[:, t0:t0 + w].rearrange("p a b -> p (a b)"), start=True,
                              stop=True).then_inc(pe_done, pe_(f"B rot {j}"))

                def scores(b):
                    pe.wait_ge(pool_done, pool_.at(f"B x {b + 1}"))
                    if b == 0:
                        pe.wait_ge(act_done, act_.at("B kx"))
                    for h in range(4 * b, 4 * b + 4):
                        bank_free("S", h)
                        e = h % 2
                        half_ = slice(64 * e, 64 * e + 64)
                        keys = b_x[half_, 8] if h // 8 == e else b_kx[half_, :]
                        q = b_x[half_, h // 2]
                        o = ps[:, BANK["S", h], :]
                        pe.matmul(o[:, 0:P], q[:, 0:P], keys[:, 0:P], start=True, stop=True)
                        pe.matmul(o[:, P:384], q[:, P:], keys, start=True, stop=True).then_inc(pe_done, pe_(f"B s {h}"))

                def bank_free(kind, h):
                    if (kind, h) not in BEFORE:
                        evacuated(u + 4 + h)
                        return
                    before, g = BEFORE[kind, h]
                    if before == "S":
                        pe.wait_ge(vec_done, vec.at(f"B s {g}"))
                    else:
                        pe.wait_ge(act_done, act_.at(f"B pT {g}"))

                def turn_probs(b):
                    for h in range(4 * b, 4 * b + 4):
                        bank_free("T", h)
                        pe.wait_ge(vec_done, vec.at(f"B p {h} 1"))
                        for o in (0, P, 2 * P):
                            last = pe.transpose(ps[:, BANK["T", h], o:o + P], b_s[:, h % 8, o:o + P], ident[:, :])
                        last.then_inc(pe_done, pe_(f"B pT {h}"))

                def values(b):
                    if b:
                        pe.wait_ge(vec_done, vec.at(f"B lo {b - 1}"))
                    for h in range(4 * b, 4 * b + 4):
                        pe.wait_ge(act_done, act_.at(f"B pT {h}"))
                        j, e = h // 2, h % 2
                        vh = slice(64 * (h // 8), 64 * (h // 8) + 64)
                        o = half(STAT, j)[64 * e:64 * e + 64]
                        pt = b_pt[:, h % 4]
                        pe.matmul(o[:, 0:P], b_v[:, 0, vh], pt[:, 0:P], start=True, stop=True)
                        pe.matmul(o[:, P:], b_v[:, 0, vh], pt[:, P:2 * P], start=True, stop=False, skip_group_check=True)
                        last = pe.matmul(o[:, P:], b_v[:, 1, vh], pt[:, 2 * P:], start=False, stop=True, skip_group_check=True)
                    last.then_inc(pe_done, pe_(f"B o {b}"))

                def out_unit(j):
                    k = j - 2
                    pe.wait_ge(vec_done, vec.at(f"B lo {k}" if k >= 0 else "B m lo"))
                    d_unit(v + j, y0=2 * k if k >= 0 else 8 + 2 * j, start=j == 0, norm=n + 1 if j == 5 else None)

                g_unit(u, norm=n)
                g_unit(u + 1)
                stat(n)
                g_unit(u + 2)
                evacuated(u)
                query_sums("B", xsq_b)
                g_unit(u + 3)
                mem_scores("B", xq_b)
                pe.wait_ge(vec_done, vec.at("B m max 0"))
                pe.wait_ge(act_done, act_.at("B sq 0"))
                pe.matmul(ps[:, STAT, T:], block_ones[:, :], b_sqk, start=True, stop=True).then_inc(pe_done, pe_("B sum"))
                g_unit(u + 4)
                mem_turn("B", p_b, 0, lambda: None)
                pair(0)
                g_unit(u + 5)
                mem_out("B", pt_b, 0)
                pair(1)
                pe.wait_ge(pool_done, pool_.at("B x 0"))
                for kt in range(2):
                    pe.transpose(ps[:, STAT, kt * P:kt * P + P], b_x[:, 9, kt * P:kt * P + P], ident[:, :])
                pe.matmul(ps[:, STAT, T:], swap[:, :], b_x[:, 8], start=True, stop=True).then_inc(pe_done, pe_("B k v"))
                g_unit(u + 6)
                pair(2)
                pair(3)
                scores(0)
                pair(4)
                for t in range(8):
                    pe.wait_ge(act_done, act_.at(f"B sq {t // 2 + 1}"))
                    last = pe.matmul(ps[0:16, STAT, 0:T], pair_rows[:, 16 - 2 * t:32 - 2 * t], b_sq_tiles[:, t], start=t == 0, stop=t == 7)
                last.then_inc(pe_done, pe_("B qsum"))
                pe.wait_ge(vec_done, vec.at("B qsum"))
                for tt in range(2):
                    last = pe.transpose(ps[:, STAT, T + 16 * tt:T + 16 * tt + 16], b_rows[:, tt * P:tt * P + P], ident[0:16, 0:16])
                last.then_inc(pe_done, pe_("B qcol"))
                pe.wait_ge(vec_done, vec.at("B sin 4"))
                out_unit(0)
                scores(1)
                turn_probs(0)
                values(0)
                out_unit(1)
                turn_probs(1)
                values(1)
                scores(2)
                scores(3)
                out_unit(2)
                out_unit(3)
                for b in (2, 3):
                    turn_probs(b)
                    values(b)
                    out_unit(b + 2)

            def ssd(n):
                g_unit(U["dt"], offs=(0,), norm=n)

                def columns():
                    pe.wait_ge(vec_done, vec.at("S cross"))
                    for k, r in enumerate((s_dth[:, 0:P], s_dth[:, P:], s_nA[:, 0:P], s_nA[:, P:], s_cross[:, 0:P])):
                        last = pe.transpose(ps[:, STAT, 32 * k:32 * k + 32], r, ident[0:32, 0:32])
                    last.then_inc(pe_done, pe_("S cols"))

                def products(half_):
                    pe.wait_ge(pool_done, pool_.at(f"S x {2 + half_}"))
                    for g in (2 * half_, 2 * half_ + 1):
                        b, c = s_x[:, 16 + g], s_x[:, 20 + g]
                        pe.matmul(ps[:, g, 0:T], b[:, 0:P], c, start=True, stop=True)
                        pe.matmul(ps[:, g, T:384], b[:, P:], c[:, P:], start=True, stop=True).then_inc(pe_done, pe_(f"S CB {g}"))

                def x_turned(j):
                    pe.wait_ge(pool_done, pool_.at(f"S x {j + 4}"))
                    pe.wait_ge(vec_done, vec.at(f"S xdt {j - 1} 1" if j else "S bias_col"))
                    for tt in range(2):
                        for t in range(2):
                            last = pe.transpose(ps[:, STAT, tt * T + t * P:tt * T + t * P + P], s_x[:, 2 * j + t, tt * P:tt * P + P], ident[:, :])
                    last.then_inc(pe_done, pe_(f"S xT {j}"))

                def decays(j):
                    for h in range(4 * j, 4 * j + 4):
                        if j:
                            pe.wait_ge(act_done, act_.at(f"S e {(h - 4) | 1} 1"))
                        else:
                            pe.wait_ge(vec_done, vec.at("S CB 1"))
                        pick = select[:, h:h + 1].broadcast_to([32, P])
                        pe.matmul(half(h % 4 // 2, h), pick, A_hi, start=True, stop=False, skip_group_check=True)
                        pe.matmul(half(h % 4 // 2, h), pick, A_lo, start=False, stop=True, skip_group_check=True).then_inc(pe_done, pe_(f"S A {h}"))

                def scan(j):
                    if j < 2:
                        pe.wait_ge(vec_done, vec.at("S CB 3"))
                    else:
                        pe.wait_ge(vec_done, vec.at(f"S y {2 * j - 3}"))
                    pe.wait_ge(vec_done, vec.at(f"S xdt {j} 1"))
                    for h in range(4 * j, 4 * j + 4):
                        pe.wait_ge(pool_done, pool_.at(f"S s {h}"))
                        e, t = h % 2, h % 4 // 2
                        o = ps[64 * e:64 * e + 64, 2 + j % 2, t * T:t * T + T]
                        w = s_e[:, h % 6]
                        pe.matmul(o, s_xdt[:, 0, 64 * h:64 * h + 64], w[:, 0:T], start=True, stop=False, skip_group_check=True)
                        pe.matmul(o[:, P:], s_xdt[:, 1, 64 * h:64 * h + 64], w[:, T:], start=False, stop=True,
                                  skip_group_check=True).then_inc(pe_done, pe_(f"S y {h}"))

                def z_sum(i):
                    if i == 0:
                        pe.wait_ge(vec_done, vec.at("S xdt 7 1"))
                    if i == 4:
                        pe.wait_ge(act_done, act_.at("S e 31 1"))
                    pe.wait_ge(pool_done, pool_.at(f"S zsq {i}"))
                    pe.matmul(half(STAT if i < 4 else 1, i // 2), ones[:, :], s_zsq[:, i % 2], start=i % 2 == 0,
                              stop=i % 2 == 1, skip_group_check=True).then_inc(pe_done, pe_(f"S zsum {i}"))

                for c in range(20):
                    g_unit(U["bc"] + c)
                    if c == 0:
                        stat(n)
                    if c == 3:
                        columns()
                    if c in (6, 7):
                        products(c - 6)
                    if 10 <= c < 18:
                        scan(c - 10)
                    if 8 <= c < 16:
                        decays(c - 8)
                        x_turned(c - 8)
                    if c > 15:
                        z_sum(c - 16)
                for j in range(4):
                    g_unit(U["ga"] + j)
                    z_sum(4 + j)
                for j in range(4):
                    g_unit(U["gb"] + j)
                for j in range(4):
                    k = U["aproj"] + 2 * j
                    pe.wait_ge(vec_done, vec.at("S lo 7"))
                    g_unit(k, X=(y_hi, y_lo))
                    pe.wait_ge(vec_done, vec.at("S lo 15"))
                    g_unit(k + 1, X=(y_hi, y_lo), kt0=8, into=k, opens=False)
                for j in range(12):
                    g_unit(U["sconv"] + j)
                for j in range(4):
                    g_unit(U["sproj"] + j, X=(y_hi, y_lo), ready=lambda k: pe.wait_ge(vec_done, vec.at(f"S slo {k // 2}")))
                for j in range(4):
                    pe.wait_ge(vec_done, vec.at(f"S mlo {j}"))
                    d_unit(U["w_o"] + j, Y=(xg_hi, xg_lo), y0=2 * j, start=j == 0, norm=n + 1 if j == 3 else None)

            pe.wait_ge(pool_done, pool_.at("ident"))
            pe.wait_ge(gain_loaded, 16)
            pe.transpose(ps[:, STAT, 0:8], rows[0:8, 0, :], ident[0:8, 0:8]).then_inc(pe_done, pe_("mem gain"))
            pe.wait_ge(mem_loaded, 16)
            turn(memin, 0)
            for name, _, _ in PHASES:
                n = norm_of[name][0]
                if name.startswith("ffn"):
                    ffn(int(name[3:]), n)
                elif name != "final":
                    {"mem": mem, "mixa": mixa, "mixb": mixb, "ssd": ssd}[name](n)
            for k in range(DT):
                pe.wait_ge(vec_done, vec.at(f"x gain {k}"))
                for tt in range(2):
                    last = pe.transpose(ps[:, 2 * tt + k // 4, (k % 4) * P:(k % 4) * P + P], x_gain[:, k, tt * P:tt * P + P], ident[:, :])
            last.then_inc(pe_done, pe_("out"))
            pe.wait_ge(squared, 4 * norm_of["final"][0] + 4)
            for tt in range(2):
                for k in range(DT):
                    last = pe.matmul(ps[:, STAT, tt:tt + 1], tiles(sq[:, k // 2])[:, k % 2, tt * P:tt * P + P], ones[:, 0:1],
                                     start=k == 0, stop=k == DT - 1, skip_group_check=True)
            last.then_inc(stat_done, 1)

    return {e: c.found for e, c in counts.items()}


def constants():
    half = B_HD // 8
    freq = (np.float32(500000.0) ** (-np.arange(0, 2 * half, 2, dtype=np.float32) / np.float32(2 * half))).astype(np.float32)
    per_head = np.concatenate([freq, freq, np.zeros(B_HD - 2 * half, np.float32)])
    return {"inv_freq": np.ascontiguousarray(np.tile(per_head, 2)[:, None])}


def kernel(**inputs):
    from concourse import bacc
    from concourse.bass_utils import run_bass_kernel_spmd

    arrays = {f"in_{name}_dram": np.ascontiguousarray(v) for name, v in {**inputs, **constants()}.items()}

    def program(known):
        nc = bacc.Bacc("TRN2", target_bir_lowering=False, num_devices=1)
        a = {name[3:-5]: nc.dram_tensor(name, v.shape, mybir.dt.from_np(v.dtype), kind="ExternalInput").ap()
             for name, v in arrays.items()}
        out = nc.dram_tensor("out_0_dram", (1, T, D), F32, kind="ExternalOutput").ap()
        return nc, build(nc, a, out, known)

    _, marks = program(None)
    nc, _ = program(marks)
    return run_bass_kernel_spmd(nc, [arrays], core_ids=[0]).results[0]["out_0_dram"]
```
